# Optimizing a Trainium2 kernel written in Bass

```python
import jax, jax.numpy as jnp
from jax import lax
import numpy as np
import math

D_MODEL = 2048
BATCH = 1
SEQ = 256
DEPTH = 1

CHUNK = 64
D_MIX = D_MODEL
D_A = D_MIX // 2
D_B = D_MIX - D_A
GROUP_DIM = 64
N_GROUPS_A = D_A // GROUP_DIM
N_GROUPS_B = D_B // GROUP_DIM
CONV_A_WIDTH = 3
CONV_B_WIDTH = 31
D_IN = 3 * D_A + 2 * D_B
D_FF = 4 * D_MODEL
EPS = 1e-6


def rms_norm(x, gain):
    xf = x.astype(jnp.float32)
    y = xf * lax.rsqrt(jnp.mean(xf * xf, axis=-1, keepdims=True) + EPS)
    return (y * gain.astype(jnp.float32)).astype(x.dtype)

def layer_norm(x, gain, bias):
    xf = x.astype(jnp.float32)
    mu = jnp.mean(xf, axis=-1, keepdims=True)
    var = jnp.mean(jnp.square(xf - mu), axis=-1, keepdims=True)
    y = (xf - mu) * lax.rsqrt(var + EPS)
    return (y * gain.astype(jnp.float32) + bias.astype(jnp.float32)).astype(x.dtype)

def causal_dwconv(u, w):
    k, c = w.shape
    return lax.conv_general_dilated(
        u, w[:, None, :].astype(u.dtype),
        window_strides=(1,),
        padding=[(k - 1, 0)],
        dimension_numbers=("NWC", "WIO", "NWC"),
        feature_group_count=c,
    )

def first_inputs(seed: int = 0) -> dict:
    key = jax.random.key(seed)
    ks = jax.random.split(key, 16)
    f32 = jnp.float32

    def normal(k, shape, scale):
        return jax.random.normal(k, shape, f32) * scale

    def gain(k, n):
        return jnp.ones((DEPTH, n), f32) + normal(k, (DEPTH, n), 0.02)

    return {
        "x": normal(ks[0], (BATCH, SEQ, D_MODEL), 1.0),
        "mix_pre_gain": gain(ks[1], D_MODEL),
        "w_in": normal(ks[2], (DEPTH, D_MODEL, D_IN), D_MODEL ** -0.5),
        "conv_a_w": normal(ks[3], (DEPTH, CONV_A_WIDTH, D_A), CONV_A_WIDTH ** -0.5),
        "conv_b_w": normal(ks[4], (DEPTH, CONV_B_WIDTH, D_B), CONV_B_WIDTH ** -0.5),
        "conv_b_bias": normal(ks[5], (DEPTH, D_B), 0.02),
        "ln_b_gain": gain(ks[6], D_B),
        "ln_b_bias": normal(ks[7], (DEPTH, D_B), 0.02),
        "w_out": normal(ks[8], (DEPTH, D_MIX, D_MODEL), D_MIX ** -0.5),
        "mix_post_gain": gain(ks[9], D_MODEL),
        "mlp_pre_gain": gain(ks[10], D_MODEL),
        "w_up": normal(ks[11], (DEPTH, D_MODEL, D_FF), D_MODEL ** -0.5),
        "w_down": normal(ks[12], (DEPTH, D_FF, D_MODEL), D_FF ** -0.5),
        "mlp_post_gain": gain(ks[13], D_MODEL),
    }

def first_block(x, mix_pre_gain, w_in, conv_a_w, conv_b_w, conv_b_bias, ln_b_gain,
              ln_b_bias, w_out, mix_post_gain, mlp_pre_gain, w_up, w_down,
              mlp_post_gain):
    h = x
    for l in range(DEPTH):
        u = rms_norm(h, mix_pre_gain[l])
        p = jnp.einsum("bsd,de->bse", u, w_in[l])
        b_gate, c_gate, v_a, val_b, gate_b = jnp.split(
            p, [D_A, 2 * D_A, 3 * D_A, 3 * D_A + D_B], axis=-1)

        y_a = b_gate * causal_dwconv(c_gate * v_a, conv_a_w[l])

        g = val_b * jax.nn.sigmoid(gate_b)
        g = causal_dwconv(g, conv_b_w[l]) + conv_b_bias[l].astype(g.dtype)
        y_b = jax.nn.silu(layer_norm(g, ln_b_gain[l], ln_b_bias[l]))

        mixed = jnp.concatenate([y_a, y_b], axis=-1)
        o = jnp.einsum("bse,ed->bsd", mixed, w_out[l])
        h = h + rms_norm(o, mix_post_gain[l])

        m = rms_norm(h, mlp_pre_gain[l])
        z = jnp.square(jax.nn.relu(jnp.einsum("bsd,df->bsf", m, w_up[l])))
        z = jnp.einsum("bsf,fd->bsd", z, w_down[l])
        h = h + rms_norm(z, mlp_post_gain[l])
    return h


HEAD_DIM = 128
H_A = 4
H_B = 6
H_C = 6
N_HEADS = H_A + H_B + H_C
H_SOFT = H_B + H_C
MIX_WIDTH = N_HEADS * HEAD_DIM
N_BRANCH = 3
D_FF_2 = -(-(8 * D_MODEL) // (3 * 256)) * 256
Q_BLOCK = 128
MOBA_BLOCK = 256
MOBA_TOPK = 3
MOBA_Q_CHUNK = 32
DILATIONS = ((128, 1), (512, 4), (2048, 16))
BAND_BLOCK = 128
N_BUCKETS = 32
MAX_DISTANCE = 2048
RMS_EPS = 1e-6
NEG_INF = -1e30


def rmsnorm(x, g):
    xf = x.astype(jnp.float32)
    y = xf * lax.rsqrt(jnp.mean(xf * xf, axis=-1, keepdims=True) + RMS_EPS)
    return (y * g.astype(jnp.float32)).astype(x.dtype)

def t5_bucket(dist):
    max_exact = N_BUCKETS // 2
    d = jnp.maximum(dist, 0)
    df = jnp.maximum(d, 1).astype(jnp.float32)
    large = max_exact + (jnp.log(df / max_exact) / math.log(MAX_DISTANCE / max_exact)
                         * (N_BUCKETS - max_exact)).astype(jnp.int32)
    large = jnp.minimum(large, N_BUCKETS - 1)
    return jnp.where(d < max_exact, d, large)

def stick_breaking_attention(q, k, v):
    B, H, S, hd = q.shape
    scale = hd ** -0.5
    kpos = jnp.arange(S)

    def block(i):
        t0 = i * Q_BLOCK
        qb = lax.dynamic_slice_in_dim(q, t0, Q_BLOCK, axis=2)
        z = jnp.einsum('bhqd,bhkd->bhqk', qb, k).astype(jnp.float32) * scale
        qpos = t0 + jnp.arange(Q_BLOCK)
        past = kpos[None, :] < qpos[:, None]
        log_beta = jax.nn.log_sigmoid(z)
        log_1mb = jnp.where(past, jax.nn.log_sigmoid(-z), 0.0)
        after = lax.cumsum(log_1mb, axis=3, reverse=True) - log_1mb
        w = jnp.where(past, jnp.exp(log_beta + after), 0.0)
        return jnp.einsum('bhqk,bhkd->bhqd', w.astype(v.dtype), v)

    out = lax.map(block, jnp.arange(S // Q_BLOCK))
    return jnp.moveaxis(out, 0, 2).reshape(B, H, S, hd)

def moba_attention(q, k, v, bias_table):
    B, H, S, hd = q.shape
    nb = -(-S // MOBA_BLOCK)
    s_pad = nb * MOBA_BLOCK
    pad = ((0, 0), (0, 0), (0, s_pad - S), (0, 0))
    kp, vp = jnp.pad(k, pad), jnp.pad(v, pad)
    kblk = kp.reshape(B, H, nb, MOBA_BLOCK, hd)
    vblk = vp.reshape(B, H, nb, MOBA_BLOCK, hd)
    scale = hd ** -0.5
    bias_hb = bias_table.T.astype(jnp.float32)
    n_sel = min(MOBA_TOPK, nb - 1)
    own_blk = jnp.arange(S) // MOBA_BLOCK
    if n_sel > 0:
        kmean = jnp.mean(kblk, axis=3)
        gate = jnp.einsum('bhsd,bhnd->bhsn', q, kmean).astype(jnp.float32)
        fully_past = jnp.arange(nb)[None, :] < own_blk[:, None]
        gate = jnp.where(fully_past, gate, NEG_INF)
        _, sel = lax.top_k(gate, n_sel)
        sel_ok = sel < own_blk[:, None]
    b_idx = jnp.arange(B)[:, None, None, None]
    h_idx = jnp.arange(H)[None, :, None, None]
    in_blk = jnp.arange(MOBA_BLOCK)

    def chunk(i):
        t0 = i * MOBA_Q_CHUNK
        qc = lax.dynamic_slice_in_dim(q, t0, MOBA_Q_CHUNK, axis=2)
        tq = t0 + jnp.arange(MOBA_Q_CHUNK)
        b0 = (t0 // MOBA_BLOCK) * MOBA_BLOCK
        k_own = lax.dynamic_slice_in_dim(kp, b0, MOBA_BLOCK, axis=2)
        v_own = lax.dynamic_slice_in_dim(vp, b0, MOBA_BLOCK, axis=2)
        dist = tq[:, None] - (b0 + in_blk)[None, :]
        l_own = jnp.einsum('bhqd,bhkd->bhqk', qc, k_own).astype(jnp.float32) * scale
        l_own = jnp.where(dist >= 0, l_own + bias_hb[:, t5_bucket(dist)], NEG_INF)
        if n_sel == 0:
            p = jax.nn.softmax(l_own, axis=-1).astype(v.dtype)
            return jnp.einsum('bhqk,bhkd->bhqd', p, v_own)
        sc = lax.dynamic_slice_in_dim(sel, t0, MOBA_Q_CHUNK, axis=2)
        ok = lax.dynamic_slice_in_dim(sel_ok, t0, MOBA_Q_CHUNK, axis=2)
        k_sel = kblk[b_idx, h_idx, sc]
        v_sel = vblk[b_idx, h_idx, sc]
        dist_sel = tq[:, None, None] - (sc[..., None] * MOBA_BLOCK + in_blk)
        l_sel = jnp.einsum('bhqd,bhqnkd->bhqnk', qc, k_sel).astype(jnp.float32) * scale
        l_sel = l_sel + bias_hb[h_idx[..., None], t5_bucket(dist_sel)]
        n_past = n_sel * MOBA_BLOCK
        l_sel = jnp.where(ok[..., None], l_sel, NEG_INF).reshape(B, H, MOBA_Q_CHUNK, n_past)
        p = jax.nn.softmax(jnp.concatenate([l_sel, l_own], axis=-1), axis=-1).astype(v.dtype)
        o = jnp.einsum('bhqk,bhqkd->bhqd', p[..., :n_past],
                       v_sel.reshape(B, H, MOBA_Q_CHUNK, n_past, hd))
        return o + jnp.einsum('bhqk,bhkd->bhqd', p[..., n_past:], v_own)

    out = lax.map(chunk, jnp.arange(S // MOBA_Q_CHUNK))
    return jnp.moveaxis(out, 0, 2).reshape(B, H, S, hd)

def dilated_attention(q, k, v, bias_table):
    B, H, S, hd = q.shape
    scale = hd ** -0.5
    bb = BAND_BLOCK
    qi = jnp.arange(bb)[:, None]
    kj = jnp.arange(2 * bb)[None, :]
    delta = qi + bb - kj
    outs, lses = [], []
    for window, r in DILATIONS:
        span = window // r
        L = S // r
        nb = -(-L // bb)
        Lp = nb * bb

        def to_sub(t):
            t = t.reshape(B, H, L, r, hd).swapaxes(2, 3)
            return jnp.pad(t, ((0, 0), (0, 0), (0, 0), (0, Lp - L), (0, 0)))

        def band(t):
            t = jnp.pad(to_sub(t), ((0, 0), (0, 0), (0, 0), (bb, 0), (0, 0))).reshape(B, H, r, nb + 1, bb, hd)
            return jnp.concatenate([t[:, :, :, :-1], t[:, :, :, 1:]], axis=4)

        qs = to_sub(q).reshape(B, H, r, nb, bb, hd)
        kb, vb = band(k), band(v)
        key_idx = (jnp.arange(nb)[:, None, None] - 1) * bb + kj[None]
        mask = (delta >= 0) & (delta <= span) & (key_idx >= 0)
        bias = jnp.transpose(bias_table[t5_bucket(delta * r)], (2, 0, 1)).astype(jnp.float32)
        logits = jnp.einsum('bhrnqd,bhrnkd->bhrnqk', qs, kb).astype(jnp.float32) * scale
        logits = jnp.where(mask, logits + bias[:, None, None], NEG_INF)
        m = jnp.max(logits, axis=-1, keepdims=True)
        p = jnp.exp(logits - m)
        den = jnp.sum(p, axis=-1, keepdims=True)
        o = jnp.einsum('bhrnqk,bhrnkd->bhrnqd', (p / den).astype(v.dtype), vb)
        lse = (m + jnp.log(den))[..., 0]

        def from_sub(t):
            t = t.reshape((B, H, r, Lp) + t.shape[5:])[:, :, :, :L]
            return jnp.swapaxes(t, 2, 3).reshape((B, H, S) + t.shape[4:])

        outs.append(from_sub(o))
        lses.append(from_sub(lse))
    w = jax.nn.softmax(jnp.stack(lses, axis=0), axis=0)
    return jnp.einsum('gbhs,gbhsd->bhsd', w.astype(v.dtype), jnp.stack(outs, axis=0))

def hybrid_layer(x, g_mix, w_in, q_gain, k_gain, w_branch, w_out, g_ffn, w_gu, w_down, rel_bias):
    B, S, _ = x.shape
    h = rmsnorm(x, g_mix)
    proj = h @ w_in
    qkv = proj[..., :3 * MIX_WIDTH].reshape(B, S, 3, N_HEADS, HEAD_DIM)
    qkv = jnp.transpose(qkv, (2, 0, 3, 1, 4))
    q, k, v = qkv[0], qkv[1], qkv[2]
    gates = jax.nn.sigmoid(proj[..., 3 * MIX_WIDTH:].astype(jnp.float32)).astype(x.dtype)
    gates = gates.reshape(B, S, N_BRANCH, D_MODEL)

    o_a = stick_breaking_attention(q[:, :H_A], k[:, :H_A], v[:, :H_A])
    qn = rmsnorm(q[:, H_A:], q_gain[:, None, :])
    kn = rmsnorm(k[:, H_A:], k_gain[:, None, :])
    o_b = moba_attention(qn[:, :H_B], kn[:, :H_B], v[:, H_A:H_A + H_B], rel_bias[:, :H_B])
    o_c = dilated_attention(qn[:, H_B:], kn[:, H_B:], v[:, H_A + H_B:], rel_bias[:, H_B:])

    def flat(o):
        return jnp.transpose(o, (0, 2, 1, 3)).reshape(B, S, -1)

    ea, eb = H_A * HEAD_DIM, (H_A + H_B) * HEAD_DIM
    merged = (gates[:, :, 0] * (flat(o_a) @ w_branch[:ea])
              + gates[:, :, 1] * (flat(o_b) @ w_branch[ea:eb])
              + gates[:, :, 2] * (flat(o_c) @ w_branch[eb:]))
    x = x + merged @ w_out

    h2 = rmsnorm(x, g_ffn)
    gu = h2 @ w_gu
    x = x + (jax.nn.silu(gu[..., :D_FF_2]) * gu[..., D_FF_2:]) @ w_down
    return x

def second_inputs(seed: int = 0) -> dict:
    key = jax.random.key(seed)
    ks = jax.random.split(key, 11)

    def nrm(k, shape, s):
        return jax.random.normal(k, shape, jnp.float32) * s

    return {
        'x': nrm(ks[0], (BATCH, SEQ, D_MODEL), 1.0),
        'g_mix': 1.0 + nrm(ks[1], (DEPTH, D_MODEL), 0.02),
        'w_in': nrm(ks[2], (DEPTH, D_MODEL, 3 * MIX_WIDTH + N_BRANCH * D_MODEL), D_MODEL ** -0.5),
        'q_gain': 1.0 + nrm(ks[3], (DEPTH, H_SOFT, HEAD_DIM), 0.02),
        'k_gain': 1.0 + nrm(ks[4], (DEPTH, H_SOFT, HEAD_DIM), 0.02),
        'w_branch': nrm(ks[5], (DEPTH, MIX_WIDTH, D_MODEL), (MIX_WIDTH / N_BRANCH) ** -0.5),
        'w_out': nrm(ks[6], (DEPTH, D_MODEL, D_MODEL), D_MODEL ** -0.5),
        'g_ffn': 1.0 + nrm(ks[7], (DEPTH, D_MODEL), 0.02),
        'w_gu': nrm(ks[8], (DEPTH, D_MODEL, 2 * D_FF_2), D_MODEL ** -0.5),
        'w_down': nrm(ks[9], (DEPTH, D_FF_2, D_MODEL), D_FF_2 ** -0.5),
        'rel_bias': nrm(ks[10], (N_BUCKETS, H_SOFT), 0.5),
    }

def second_block(x, g_mix, w_in, q_gain, k_gain, w_branch, w_out, g_ffn, w_gu, w_down, rel_bias):
    for l in range(DEPTH):
        x = hybrid_layer(x, g_mix[l], w_in[l], q_gain[l], k_gain[l], w_branch[l], w_out[l],
                         g_ffn[l], w_gu[l], w_down[l], rel_bias)
    return x


def setup_inputs(seed=0):
    out = dict(first_inputs(seed))
    for name, value in second_inputs(seed + 1).items():
        if name != "x":
            out[name + "_2"] = value
    return out


def reference(
    x, mix_pre_gain, w_in, conv_a_w, conv_b_w, conv_b_bias, ln_b_gain, ln_b_bias, w_out,
    mix_post_gain, mlp_pre_gain, w_up, w_down, mlp_post_gain, g_mix_2, w_in_2, q_gain_2,
    k_gain_2, w_branch_2, w_out_2, g_ffn_2, w_gu_2, w_down_2, rel_bias_2,
):
    x = first_block(
        x, mix_pre_gain, w_in, conv_a_w, conv_b_w, conv_b_bias, ln_b_gain, ln_b_bias, w_out,
        mix_post_gain, mlp_pre_gain, w_up, w_down, mlp_post_gain,
    )
    return second_block(
        x, g_mix_2, w_in_2, q_gain_2, k_gain_2, w_branch_2, w_out_2, g_ffn_2, w_gu_2, w_down_2,
        rel_bias_2,
    )


_drawn_inputs = setup_inputs


def setup_inputs(seed=0):
    import zlib

    import numpy as np

    out = dict(_drawn_inputs(seed))
    spreads = {}
    factors = {'ln_b_gain': 5.358,
     'ln_b_bias': 6.458,
     'mix_post_gain': 3.519,
     'mlp_pre_gain': 4.043,
     'mlp_post_gain': 4.452,
     'g_mix_2': 8.0,
     'q_gain_2': 8.0,
     'k_gain_2': 8.0,
     'g_ffn_2': 6.31}
    for name, (base, spread) in spreads.items():
        noise = np.random.default_rng([zlib.crc32(name.encode()), seed]).standard_normal(out[name].shape)
        drawn = base * np.exp(spread * noise) if base else spread * noise
        out[name] = __import__('jax').numpy.asarray(drawn.astype(out[name].dtype))
    for name, factor in factors.items():
        out[name] = (out[name] * factor).astype(out[name].dtype)
    return out
```

```python
from contextlib import ExitStack

import concourse.bass as bass
import numpy as np
from concourse import mybir

F32 = mybir.dt.float32
F32R = mybir.dt.float32r
ACT = mybir.ActivationFunctionType
ALU = mybir.AluOpType
AX = mybir.AxisListType

P = 128
D = 2048
S = 256
TT = S // P
W = 512
NCH = D // W
RING = 4
KS = 2
KT = D // P
SPU = KT // KS
EPS = 1e-6

D_A = D // 2
K_A, K_B = 3, 31
CT = D_A // P
FF1 = 4 * D
FF2 = 5632
NH = 16
H_STICK, H_BLOCK, H_DIL = 4, 6, 6
H_SOFT = H_BLOCK + H_DIL
QSCALE = float(P) ** -0.5
LINE = 384

G_MIXPRE, G_MLPPRE, G_MIX2, G_FFN2 = 0, 16, 32, 48
G_CBIAS, G_LNG, G_LNB, G_CONVA = 64, 72, 80, 88
G_CONVB = 112
G_QG, G_KG = 360, 372
ROWS = (112, 124, 124, 24)

U_IN, U_OUT, U_MLP, U_QK, U_V, U_G0, U_B0, U_J, U_OUT2, U_FF = 0, 10, 14, 46, 54, 58, 61, 64, 82, 86
G_IN, G_OUT, G_MLP, G_QK, G_V, G_G0, G_B0, G_J, G_OUT2, G_FF = 0, 80, 112, 368, 432, 464, 488, 496, 592, 624
G_FF3 = G_FF + 192
G_DN3 = G_FF3 + 48
G_END = G_DN3 + 24
T_X, T_IN, T_N1, T_MLP, T_N2, T_QK, T_ATT, T_M, T_N3, T_FF = 0, 8, 20, 28, 60, 68, 84, 100, 108, 116
S_X, S_YA, S_YB, S_N1, S_MLP, S_N2, S_O, S_M, S_N3, S_FF = 0, 8, 12, 16, 24, 56, 64, 80, 88, 96
K_QK, K_ATT = 8, 24
IN_COLS = [3 * D_A, 4 * D_A, 3 * D_A + W, 4 * D_A + W, D_A, 2 * D_A, D_A + W, 2 * D_A + W, 0, W]
ATT_SLOTS = (1, 4, 6)
BR_SLOTS = (H_STICK // KS, H_BLOCK // KS, H_DIL // KS)


def build_program(nc, t):
    ctx = ExitStack()
    with ctx:
        base = -(-nc.sbuf_base // 32) * 32
        ctx.enter_context(nc.sbuf_tensor("arena", [P, 207 * 256], F32))
        

        def at(name, kb, shape, dt=F32):
            return nc.alloc_sbuf_tensor_at(name, shape, dt, offset=base + int(kb * 1024))

        def ps(name, shape):
            return ctx.enter_context(nc.psum_tensor(name, shape, F32))

        def sem(name):
            return ctx.enter_context(nc.semaphore(name))

        raw = at("raw", 0, [P, RING, KS, W])
        w_hi = at("w_hi", 16, [P, RING, KS, W], F32R)
        w_lo = at("w_lo", 32, [P, RING, KS, W], F32R)
        a_hi = at("a_hi", 48, [P, KT, S], F32R)
        a_lo = at("a_lo", 64, [P, KT, S], F32R)
        b_hi = at("b_hi", 80, [P, KT, S], F32R)
        b_lo = at("b_lo", 96, [P, KT, S], F32R)
        rows = at("rows", 112, [P, 4, P])
        onehot = at("onehot", 114, [32, LINE])
        lmask = at("lmask", 116, [H_SOFT, LINE])
        line = at("line", 118, [H_SOFT, LINE])
        relb = at("relb", 120, [32, H_SOFT])
        conva = at("conva", 112, [P, CT, S])
        yt = at("yt", 120, [P, 2, 2, S])
        wide = at("wide", 112, [P, TT, NCH, W])
        vv = at("vv", 112, [P, TT, D])
        h = at("h", 128, [P, TT, NCH, W])
        gT = at("gT", 144, [P, CT, K_B - 1 + S])
        sq = at("sq", 144, [P, CT, S])
        cvT = at("cvT", 153.5, [P, CT, K_A - 1 + S])
        convb = at("convb", 162, [P, CT, S])
        dg = at("dg", 170, [P, TT, P])
        yb = at("yb", 153.5, [P, CT, S])
        qkT = at("qkT", 144, [P, 2 * NH, S])
        m_hi = at("m_hi", 144, [P, KT, S], F32R)
        m_lo = at("m_lo", 160, [P, KT, S], F32R)
        gain = at("gain", 176, [P, D])
        gate = at("gate", 176, [P, 3, TT, W])
        ev = at("ev", 188, [P, 2, TT, W])
        zz = at("zz", 196, [P, TT, W])
        bias = at("bias", 188, [P, 2, S])
        cnt = at("cnt", 190, [P, 3 * P])
        past = at("past", 191.5, [P, S])
        tri = at("tri", 192.5, [P, P])
        x0 = at("x0", 193, [P, 3 * P])
        x1 = at("x1", 194.5, [P, 3 * P])
        x2 = at("x2", 196, [P, 3 * P])
        pT = at("pT", 197.5, [P, 3 * P])
        ident = at("ident", 200, [P, P])
        mean_w = at("mean_w", 200.5, [P, P])
        ones = at("ones", 201, [P, P])
        cols = at("cols", 201.5, [P, 3 * P])
        junk = at("junk", 203, [P, TT, W], mybir.dt.bfloat16)
        ssq = at("ssq", 205, [P, 6, TT, NCH])
        rs = at("rs", 205.25, [P, 6, TT])
        ms = at("ms", 205.375, [P, 6, TT])
        half = at("half", 205.5, [P, TT])
        lnv = at("lnv", 205.53125, [P, TT])
        qkg = at("qkg", 206.125, [P, 2 * NH])
        lnr = at("lnr", 205.5625, [P, TT])
        qexp = at("qexp", 205.625, [P, 8, 8])
        qss = at("qss", 205.875, [P, 8])
        qms = at("qms", 205.90625, [P, 8])
        qrs = at("qrs", 205.9375, [P, 8])
        mx = at("mx", 206, [P, 2])
        den = at("den", 206.03125, [P, 2])
        rden = at("rden", 206.0625, [P, 2])
        nmx = at("nmx", 206.09375, [P, 2])

        acc = ps("acc", [P, 2, TT, W])
        tp = ps("tp", [P, 2, W])
        sc = ps("sc", [P, W])
        po = ps("po", [P, W])

        landed = [sem(f"landed{i}") for i in range(RING)]
        hi_ready = sem("hi_ready")
        lo_ready = sem("lo_ready")
        slot_used = sem("slot_used")
        evacuated = sem("evacuated")
        turned = sem("turned")
        split_hi = sem("split_hi")
        split_lo = sem("split_lo")
        took = sem("took")
        z_ready = sem("z_ready")
        ev_read = sem("ev_read")
        x_in = [sem(f"x_in{c}") for c in range(NCH)]
        rows_in = sem("rows_in")
        line_in = sem("line_in")
        gain1_in = sem("gain1_in")
        gain2_in = sem("gain2_in")
        line_out = sem("line_out")
        consts_in = sem("consts_in")
        bias_in = [sem("bias_in0"), sem("bias_in1")]
        out_stored = sem("out_stored")
        const_set = sem("const_set")
        cols_T = sem("cols_T")
        cols_ok = sem("cols_ok")
        squared = sem("squared")
        ssum = sem("ssum")
        rs_ok = sem("rs_ok")
        h_ready = sem("h_ready")
        step0 = sem("step0")
        conv = sem("conv")
        conv3 = sem("conv3")
        ya = sem("ya")
        ln_pe = sem("ln_pe")
        ln_dve = sem("ln_dve")
        ln_act = sem("ln_act")
        ln_pool = sem("ln_pool")
        qstep = sem("qstep")
        qpool = sem("qpool")
        folded = sem("folded")
        mstep = sem("mstep")
        gated = sem("gated")
        scored = sem("scored")
        valued = sem("valued")
        att_dve = sem("att_dve")
        att_act = sem("att_act")
        wide_zero = sem("wide_zero")

        line_dram = t["line_dram"]
        w_in = t["w_in"][0].rearrange("(k p) n -> p k n", p=P)
        w_out = t["w_out"][0].rearrange("(k p) n -> p k n", p=P)
        w_up = t["w_up"][0].rearrange("(k p) n -> p k n", p=P)
        w_down = t["w_down"][0].rearrange("(k p) n -> p k n", p=P)
        w_in2 = t["w_in_2"][0].rearrange("(k p) n -> p k n", p=P)
        w_br = t["w_branch_2"][0].rearrange("(k p) n -> p k n", p=P)
        w_out2 = t["w_out_2"][0].rearrange("(k p) n -> p k n", p=P)
        w_gu = t["w_gu_2"][0].rearrange("(k p) n -> p k n", p=P)
        w_dn2 = t["w_down_2"][0].rearrange("(k p) n -> p k n", p=P)
        x_v = t["x"][0].rearrange("(t p) (c n) -> p t c n", p=P, n=W)
        out_v = t["out"][0].rearrange("(t p) (c n) -> p t c n", p=P, n=W)

        att_act_at, att_dve_at = {}, {}
        n_act = n_dve = 0
        for n in range(NH + 1):
            if 1 <= n <= H_STICK:
                n_act += 1
                att_act_at["weight", n - 1] = n_act
                att_dve_at["sum", n - 1] = n_dve + 1
                n_dve += 3
                att_dve_at["weight", n - 1] = n_dve
            if n < H_STICK:
                for stage in ("abs", "exp", "log"):
                    n_act += 1
                    att_act_at[stage, n] = n_act
                for stage, ops in (("min", 1), ("logb", 1), ("log1", 1), ("masked", 2)):
                    n_dve += ops
                    att_dve_at[stage, n] = n_dve
            elif n < NH:
                n_act += 1
                att_act_at["exp", n] = n_act
                counted = (("count", 2),) if n >= H_STICK + H_BLOCK else ()
                for stage, ops in (("logits", 2), ("max", 2), ("neg", 1), *counted, ("recip", 1),
                                   ("prob", 2)):
                    n_dve += ops
                    att_dve_at[stage, n] = n_dve

        def att_points(u, i):
            if U_V + 1 <= u < U_B0 and i in ATT_SLOTS:
                return [3 * (u - U_V - 1) + ATT_SLOTS.index(i)]
            return []

        block = ctx.enter_context(nc.Block())

        @block.sync
        def _(sp):
            def load(s, g, src):
                ring = s % RING
                if g is not None:
                    sp.wait_ge(lo_ready, g - RING + 1)
                sp.dma_start(raw[:, ring, 0:src.shape[1]], src).then_inc(landed[ring], 16)

            def ks(s):
                return slice(KS * s, KS * s + KS)

            for c in range(NCH):
                sp.dma_start(h[:, :, c], x_v[:, :, c]).then_inc(x_in[c], 16)
                load(c, None, w_in[:, ks(c), IN_COLS[0]:IN_COLS[0] + W])
            for u in range(10):
                for s in range(SPU):
                    g = G_IN + u * SPU + s
                    if g >= RING:
                        load(g, g, w_in[:, ks(s), IN_COLS[u]:IN_COLS[u] + W])
            with sp.Fori(0, NCH) as j:
                src = w_out[:, :, bass.ds(sp.snap(j * W), W)]
                for s in range(SPU):
                    load(s, G_OUT + j * SPU + s, src[:, ks(s)])
            with sp.Fori(0, FF1 // D) as b:
                g = G_MLP + b * (2 * NCH * SPU)
                up = w_up[:, :, bass.ds(sp.snap(b * D), D)]
                down = w_down[:, bass.ds(sp.snap(b * KT), KT)]
                for j in range(NCH):
                    for s in range(SPU):
                        load(s, g + (j * SPU + s), up[:, ks(s), j * W:(j + 1) * W])
                for j in range(NCH):
                    for s in range(SPU):
                        load(s, g + ((NCH + j) * SPU + s), down[:, ks(s), j * W:(j + 1) * W])
            with sp.Fori(0, 3 * NCH) as j:
                src = w_in2[:, :, bass.ds(sp.snap(j * W), W)]
                for s in range(SPU):
                    load(s, G_QK + j * SPU + s, src[:, ks(s)])
            for b in range(3):
                for s in range(SPU):
                    g = G_G0 + b * SPU + s
                    load(g, g, w_in2[:, ks(s), (3 + b) * D:(3 + b) * D + W])
            for s in range(SPU):
                load(s, G_B0 + s, w_br[:, ks(s), 0:W])
            with sp.Fori(1, NCH) as j:
                g = G_J - 4 * SPU + j * (4 * SPU)
                col = sp.snap((j - 1) * W)
                for b in range(3):
                    src = w_in2[:, :, (3 + b) * D + W:(4 + b) * D][:, :, bass.ds(col, W)]
                    for s in range(SPU):
                        load(s, g + (b * SPU + s), src[:, ks(s)])
                src = w_br[:, :, W:][:, :, bass.ds(col, W)]
                for s in range(SPU):
                    load(s, g + (3 * SPU + s), src[:, ks(s)])
            with sp.Fori(0, NCH) as j:
                src = w_out2[:, :, bass.ds(sp.snap(j * W), W)]
                for s in range(SPU):
                    load(s, G_OUT2 + j * SPU + s, src[:, ks(s)])
            with sp.Fori(0, 2) as b:
                g = G_FF + b * (3 * NCH * SPU)
                col = sp.snap(b * D)
                halves = [w_gu[:, :, i * FF2:(i + 1) * FF2][:, :, bass.ds(col, D)] for i in range(2)]
                down = w_dn2[:, bass.ds(sp.snap(b * KT), KT)]
                for j in range(2 * NCH):
                    for s in range(SPU):
                        c0 = (j // 2) * W
                        load(s, g + (j * SPU + s), halves[j % 2][:, ks(s), c0:c0 + W])
                for j in range(NCH):
                    for s in range(SPU):
                        load(s, g + ((2 * NCH + j) * SPU + s), down[:, ks(s), j * W:(j + 1) * W])
            for j in range(6):
                for s in range(SPU):
                    g = G_FF3 + j * SPU + s
                    c0 = 2 * D + (j // 2) * W + (j % 2) * FF2
                    load(g, g, w_gu[:, ks(s), c0:c0 + W])
            for j in range(NCH):
                for s in range(6):
                    g = G_DN3 + 6 * j + s
                    load(g, g, w_dn2[:, 2 * KT + KS * s:2 * KT + KS * s + KS, j * W:(j + 1) * W])
            for j in range(NCH):
                sp.wait_ge(h_ready, 3 * NCH + j + 1)
                sp.dma_start(out_v[:, :, j], h[:, :, j]).then_inc(out_stored, 16)
            sp.wait_ge(out_stored, 16 * NCH)

        @block.tensor
        def _(pe):
            def slots(g0, u, s_from, s_to, hi, lo, split0=None, n=SPU, k0=0, ring0=0, pair=0):
                if s_from == 0 and not (isinstance(u, int) and u < 2):
                    pe.wait_ge(evacuated, u - 1)
                for s in range(s_from, s_to):
                    if split0 is not None:
                        pe.wait_ge(split_lo, split0 + s + 1)
                    pe.wait_ge(lo_ready, g0 + (s + 1))
                    ring = (ring0 + s) % RING
                    for k in range(KS):
                        kt = k0 + KS * s + k
                        for tk in range(TT):
                            out = acc[:, pair, tk, :]
                            xh, xl = (part[:, kt, tk * P:(tk + 1) * P] for part in (hi, lo))
                            wh, wl = w_hi[:, ring, k, :], w_lo[:, ring, k, :]
                            nc.tensor.matmul(out, xh, wl, start=s == 0 and k == 0, stop=False)
                            nc.tensor.matmul(out, xh, wh, start=False, stop=False)
                            mm = nc.tensor.matmul(out, xl, wh, start=False,
                                                  stop=s == n - 1 and k == KS - 1)
                    mm.then_inc(slot_used, 1)

            def turn(src, need, free=None):
                pe.wait_ge(*need)
                for g in range(2):
                    if free is not None:
                        pe.wait_ge(free[0], free[1] + g)
                    for k in range(2):
                        for tk in range(TT):
                            c = (2 * g + k) * P
                            tr = nc.tensor.transpose(tp[:, g, (2 * k + tk) * P:(2 * k + tk + 1) * P],
                                                     src[:, tk, c:c + P], ident[:, :])
                    tr.then_inc(turned, 1)

            pe.wait_ge(rows_in, 16 * 13)
            start = 0
            for i, n in enumerate(ROWS):
                tr = nc.tensor.transpose(sc[:, start:start + n], rows[0:n, i, :], ident[0:n, 0:n])
                start += n
            tr.then_inc(cols_T, 1)

            for c in range(NCH):
                turn(h[:, :, c, :], (x_in[c], 16), (split_lo, S_X + 2 * c - 1) if c else None)
                slots(G_IN, 0, 2 * c, 2 * c + 2, a_hi, a_lo, split0=S_X)
            pe.wait_ge(line_in, 48)
            nc.tensor.matmul(po[0:H_SOFT, 0:LINE], relb[:, :], onehot[:, :], start=True,
                             stop=True).then_inc(cols_T, 1)

            def in_product(u):
                if u in (2, 4, 6, 8):
                    i = u // 2
                    turn(zz, (z_ready, i), (took, 2 * i - 3) if i > 1 else None)
                elif u in (9, 10):
                    turn(ev[:, u % 2 ^ 1], (evacuated, u), (took, 7) if u == 9 else (ya, 1))

            for u in range(1, 10):
                slots(G_IN + u * SPU, u, 0, 2, a_hi, a_lo, pair=u % 2)
                in_product(u)
                slots(G_IN + u * SPU, u, 2, SPU, a_hi, a_lo, pair=u % 2)

            slots(G_OUT, U_OUT, 0, 2, b_hi, b_lo, split0=S_YA)
            in_product(10)
            slots(G_OUT, U_OUT, 2, 3, b_hi, b_lo, split0=S_YA)
            pe.wait_ge(conv, K_B * CT)
            for c in range(CT):
                mm = nc.tensor.matmul(sc[:, 0:S], mean_w[:, :], convb[:, c, :], start=c == 0,
                                      stop=c == CT - 1)
            mm.then_inc(ln_pe, 1)
            slots(G_OUT, U_OUT, 3, 4, b_hi, b_lo, split0=S_YA)
            pe.wait_ge(ln_act, 2)
            for tk in range(TT):
                for c in range(CT):
                    mm = nc.tensor.matmul(po[:, tk:tk + 1], sq[:, c, tk * P:(tk + 1) * P],
                                          mean_w[:, 0:1], start=c == 0, stop=c == CT - 1)
            mm.then_inc(ln_pe, 1)
            pe.wait_ge(ln_dve, 5)
            nc.tensor.matmul(sc[:, S:2 * S], ones[:, :], dg.rearrange("p t q -> p (t q)"),
                             start=True, stop=True).then_inc(ln_pe, 1)
            slots(G_OUT, U_OUT, 4, SPU, b_hi, b_lo, split0=S_YA)
            for j in range(1, NCH):
                slots(G_OUT + j * SPU, U_OUT + j, 0, SPU, b_hi, b_lo, pair=j % 2)

            def mlp_block(b, chunks_too):
                g, u, z, sp_ = (G_MLP + b * (2 * NCH * SPU), U_MLP + b * (2 * NCH), 4 + b * NCH,
                                S_MLP + b * (2 * NCH))
                for j in range(NCH):
                    gj = g + j * SPU
                    if chunks_too and j == 0:
                        for c in range(NCH):
                            turn(h[:, :, c, :], (h_ready, c + 1), (split_lo, S_N1 + 2 * c - 1))
                            if c < 2:
                                slots(gj, u, 2 * c, 2 * c + 2, a_hi, a_lo, split0=S_N1)
                        slots(gj, u, RING, SPU, a_hi, a_lo, split0=S_N1)
                        continue
                    slots(gj, u + j, 0, 2, a_hi, a_lo, pair=j % 2)
                    if j:
                        turn(zz, (z_ready, z + j), (split_lo, sp_ + 2 * j - 3))
                    slots(gj, u + j, 2, SPU, a_hi, a_lo, pair=j % 2)
                for j in range(NCH):
                    gj = g + (NCH + j) * SPU
                    split0 = sp_ if j == 0 else None
                    slots(gj, u + (NCH + j), 0, 2, b_hi, b_lo, split0=split0, pair=j % 2)
                    if j == 0:
                        turn(zz, (z_ready, z + NCH), (split_lo, sp_ + 2 * NCH - 3))
                    slots(gj, u + (NCH + j), 2, SPU, b_hi, b_lo, split0=split0, pair=j % 2)

            mlp_block(0, True)
            with pe.Fori(1, FF1 // D) as b:
                mlp_block(b, False)

            for c in range(2):
                turn(h[:, :, c, :], (h_ready, NCH + c + 1), (split_lo, S_N2 + 2 * c - 1))
                slots(G_QK, U_QK, 2 * c, min(2 * c + 2, 3), a_hi, a_lo, split0=S_N2)
            for c in range(2, NCH):
                turn(h[:, :, c, :], (h_ready, NCH + c + 1), (split_lo, S_N2 + 2 * c - 1))
            pe.wait_ge(split_lo, S_N2 + SPU)
            with pe.Fori(0, NCH) as i:
                for p_ in range(2):
                    g, u = G_QK + i * (2 * SPU) + p_ * SPU, U_QK + i * 2 + p_
                    slots(g, u, 3, SPU, a_hi, a_lo, pair=p_)
                    slots(g + SPU, u + 1, 0, 3, a_hi, a_lo, pair=p_ ^ 1)
                    turn(zz, (z_ready, i * 2 + (21 + p_)), (took, i * 4 + (K_QK + 2 * p_ - 1)))

            def q_of(n):
                return qkT[:, n, :]

            def k_of(n):
                return qkT[:, NH + n, :]

            def attend(n):
                if n < NH:
                    if n == 0:
                        pe.wait_ge(took, K_QK + 16)
                    else:
                        pe.wait_ge(att_dve, att_dve_at["log1" if n <= H_STICK else "logits", n - 1])
                    if n < H_STICK:
                        nc.tensor.matmul(sc[:, 0:S], k_of(n)[:, 0:P], q_of(n), start=True, stop=True)
                        mm = nc.tensor.matmul(sc[:, S:S + P], k_of(n)[:, P:S], q_of(n)[:, P:S],
                                              start=True, stop=True)
                    else:
                        nc.tensor.matmul(sc[:, 0:S], q_of(n)[:, P:S], k_of(n), start=True, stop=True)
                        mm = nc.tensor.matmul(sc[:, S:S + P], q_of(n)[:, 0:P], k_of(n)[:, 0:P],
                                              start=True, stop=True)
                    mm.then_inc(scored, 1)
                m = n - 1
                if 0 <= m < H_STICK:
                    if m == 0:
                        pe.wait_ge(consts_in, 48)
                    pe.wait_ge(att_dve, att_dve_at["masked", m])
                    after = tp[:, m % 2, :]
                    nc.tensor.matmul(after[:, 0:S], tri[:, :], x2[:, 0:S], start=True, stop=False)
                    nc.tensor.matmul(after[:, P:S], ones[:, :], x2[:, S:S + P], start=False,
                                     stop=True)
                    nc.tensor.matmul(after[:, S:S + P], tri[:, :], x2[:, S:S + P], start=True,
                                     stop=True).then_inc(turned, 1)
                elif H_STICK <= m < NH:
                    pe.wait_ge(att_dve, att_dve_at["prob", m])
                    for to, frm in ((0, S), (P, 0), (S, P)):
                        tr = nc.tensor.transpose(tp[:, m % 2, to:to + P], x2[:, frm:frm + P],
                                                 ident[:, :])
                    tr.then_inc(turned, 1)
                m = n - 2
                if m >= 0:
                    if m % 4 == 0:
                        pe.wait_ge(evacuated, U_V + m // 4 + 1)
                    if m < H_STICK:
                        pe.wait_ge(att_dve, att_dve_at["weight", m])
                    else:
                        pe.wait_ge(took, K_ATT + m - H_STICK + 1)
                    pe.wait_ge(split_lo, S_O + m)
                    nc.tensor.matmul(po[:, 0:S], vv[:, 0, m * P:(m + 1) * P], pT[:, 0:S],
                                     start=True, stop=False)
                    nc.tensor.matmul(po[:, P:S], vv[:, 1, m * P:(m + 1) * P], pT[:, S:S + P],
                                     start=False, stop=True).then_inc(valued, 1)

            for u in range(U_V, U_B0):
                g = G_V + (u - U_V) * SPU
                for s in range(3 if u == U_V else 0, SPU):
                    slots(g, u, s, s + 1, a_hi, a_lo, pair=u % 2)
                    for n in att_points(u, s):
                        attend(n)

            def branches(g, u, ring0, pair0, last):
                s0 = 0
                for b, n in enumerate(BR_SLOTS):
                    slots(g + s0, u + b, 0, n, b_hi, b_lo, n=n, k0=KS * s0, ring0=ring0 + s0,
                          pair=(pair0 + b) % 2)
                    s0 += n

            pe.wait_ge(split_lo, S_O + NH)
            branches(G_B0, U_B0, 0, U_B0 % 2, False)
            with pe.Fori(1, NCH) as j:
                g, u = G_J - 4 * SPU + j * (4 * SPU), U_J - 6 + j * 6
                for b in range(3):
                    slots(g + b * SPU, u + b, 0, 2, a_hi, a_lo, pair=b % 2)
                    if b == 0:
                        turn(zz, (z_ready, j + 28), (split_lo, S_M - 3 + j * 2))
                    slots(g + b * SPU, u + b, 2, SPU, a_hi, a_lo, pair=b % 2)
                branches(g + 3 * SPU, u + 3, 0, 1, False)

            for j in range(NCH):
                split0 = S_M if j == 0 else None
                slots(G_OUT2 + j * SPU, U_OUT2 + j, 0, 2, m_hi, m_lo, split0=split0, pair=j % 2)
                if j == 0:
                    turn(zz, (z_ready, 32), (split_lo, S_M + 5))
                else:
                    turn(h[:, :, j - 1, :], (h_ready, 2 * NCH + j), (split_lo, S_N3 + 2 * j - 3))
                slots(G_OUT2 + j * SPU, U_OUT2 + j, 2, SPU, m_hi, m_lo, split0=split0, pair=j % 2)
            turn(h[:, :, 3, :], (h_ready, 3 * NCH), (split_lo, S_N3 + 5))
            pe.wait_ge(split_lo, S_N3 + SPU)

            def ff_block(g, u, z, sp_, pairs, down_slots, ring):
                for j in range(2 * pairs):
                    slots(g + j * SPU, u + j, 0, 2, a_hi, a_lo, pair=j % 2)
                    if j and j % 2 == 0:
                        turn(zz, (z_ready, z + j // 2), (split_lo, sp_ + j - 3))
                    slots(g + j * SPU, u + j, 2, SPU, a_hi, a_lo, pair=j % 2)
                gd, ud = g + 2 * pairs * SPU, u + 2 * pairs
                for j in range(NCH):
                    split0 = sp_ if j == 0 else None
                    kw = dict(split0=split0, n=down_slots, pair=j % 2, ring0=j * down_slots)
                    slots(gd + j * down_slots, ud + j, 0, 2, b_hi, b_lo, **kw)
                    if j == 0:
                        turn(zz, (z_ready, z + pairs), (split_lo, sp_ + 2 * pairs - 3))
                    slots(gd + j * down_slots, ud + j, 2, down_slots, b_hi, b_lo, **kw)

            with pe.Fori(0, 2) as b:
                ff_block(G_FF + b * (3 * NCH * SPU), U_FF + b * (3 * NCH), 32 + b * NCH,
                         S_FF + b * (2 * NCH), NCH, SPU, 0)
            ff_block(G_FF3, U_FF + 6 * NCH, 32 + 2 * NCH, S_FF + 4 * NCH, 3, 6, 0)

        @block.scalar
        def _(act):
            def ticks(g0, s_from, s_to, ring0=0):
                for s in range(s_from, s_to):
                    ring = (ring0 + s) % RING
                    if isinstance(g0, int):
                        act.wait_ge(landed[ring], 16 * ((g0 + s) // RING + 1))
                        if g0 + s >= RING:
                            act.wait_ge(slot_used, g0 + s - RING + 1)
                    else:
                        act.wait_ge(landed[ring], g0 * 4 + 16 * (s // RING + 1))
                        act.wait_ge(slot_used, g0 + (s - RING + 1))
                    nc.scalar.activation(w_hi[:, ring], raw[:, ring], ACT.Copy).then_inc(hi_ready, 1)

            def evacuate(u, used, dst, n=None, func=ACT.Copy):
                pair = u % 2 if isinstance(u, int) else u[1]
                act.wait_ge(slot_used, used)
                if n is None:
                    nc.scalar.activation(dst, acc[:, pair], func).then_inc(evacuated, 1)
                    return
                for tk in range(TT):
                    a_ = nc.scalar.activation(dst[:, tk], acc[:, pair, tk], func,
                                              scale=rs[:, n, tk:tk + 1])
                a_.then_inc(evacuated, 1)

            def split(turned0, dst, k0, gain0=None, groups=2):
                for g in range(groups):
                    act.wait_ge(turned, turned0 + (g + 1))
                    if gain0 is None:
                        nc.scalar.activation(dst[:, bass.ds(k0 + 2 * g, 2), :].rearrange(
                            "p k s -> p (k s)"), tp[:, g, :], ACT.Copy).then_inc(split_hi, 1)
                        continue
                    for k in range(2):
                        kt = k0 + 2 * g + k
                        a_ = nc.scalar.activation(dst[:, kt, :], tp[:, g, k * S:(k + 1) * S], ACT.Copy,
                                                  scale=cols[:, gain0 + kt:gain0 + kt + 1])
                    a_.then_inc(split_hi, 1)

            def squares(n, c, src, before):
                for tk in range(TT):
                    if not (isinstance(before, int) and before + tk < 2):
                        act.wait_ge(squared, before + (tk - 1))
                    nc.scalar.activation(junk[:, tk], src[:, tk], ACT.Square,
                                         accum_out=ssq[:, n, tk, c:c + 1]).then_inc(squared, 1)

            small = ((0, 0, "mix_pre_gain", KT), (0, 16, "mlp_pre_gain", KT), (0, 32, "g_mix_2", KT),
                     (0, 48, "g_ffn_2", KT), (0, 64, "conv_b_bias", CT), (0, 72, "ln_b_gain", CT),
                     (0, 80, "ln_b_bias", CT), (0, 88, "conv_a_w", K_A * CT))
            act.dma_start(ident[:, :], t["ident"]).then_inc(rows_in, 16)
            for i, r0, name, n in small:
                src = t[name][0]
                src = (src.rearrange("(c p) -> c p", p=P) if len(src.shape) == 1
                       else src.rearrange("k (c p) -> (k c) p", p=P))
                act.dma_start(rows[r0:r0 + n, i, :], src).then_inc(rows_in, 16)
            taps = t["conv_b_w"][0].rearrange("k (c p) -> (k c) p", p=P)
            for i in range(2):
                act.dma_start(rows[0:124, 1 + i, :], taps[124 * i:124 * (i + 1), :]).then_inc(rows_in, 16)
            act.dma_start(rows[0:H_SOFT, 3, :], t["q_gain_2"][0]).then_inc(rows_in, 16)
            act.dma_start(rows[H_SOFT:2 * H_SOFT, 3, :], t["k_gain_2"][0]).then_inc(rows_in, 16)
            act.dma_start(onehot[:, :], t["onehot"]).then_inc(line_in, 16)
            act.dma_start(lmask[:, :], t["lmask"]).then_inc(line_in, 16)
            act.dma_start(relb[:, :], t["rel_bias_2"]).then_inc(line_in, 16)

            act.wait_ge(cols_ok, 1)
            for c in range(NCH):
                split(T_X + 2 * c, a_hi, 4 * c, G_MIXPRE)
                ticks(G_IN, 2 * c, 2 * c + 2)
            for c in range(NCH):
                squares(0, c, h[:, :, c], 2 * c)

            for u in range(10):
                ticks(G_IN + u * SPU, RING if u else SPU, RING + SPU)
                if u == 0:
                    act.wait_ge(rs_ok, 1)
                if u in (2, 4, 6, 8):
                    act.wait_ge(z_ready, u // 2)
                gates = u in (1, 3)
                evacuate(u, G_IN + (u + 1) * SPU, ev[:, u % 2], 0, ACT.Sigmoid if gates else ACT.Copy)
                if u % 2 and u < 8:
                    i = u // 2
                    dst, pad, c0 = (gT, K_B - 1, 4 * i) if i < 2 else (cvT, K_A - 1, 4 * (i - 2))
                    if i in (0, 2):
                        act.wait_ge(const_set, 1)
                    for g in range(2):
                        act.wait_ge(turned, T_IN + 2 * i + g + 1)
                        nc.scalar.activation(dst[:, c0 + 2 * g:c0 + 2 * g + 2, pad:pad + S],
                                             tp[:, g, :].rearrange("p (c s) -> p c s", c=2),
                                             ACT.Copy).then_inc(took, 1)
                if u >= 8:
                    for g in range(2):
                        act.wait_ge(ya, 2 * (u - 8) + g + 1)
                        k0 = 4 * (u - 8) + 2 * g
                        nc.scalar.activation(b_hi[:, k0:k0 + 2, :], yt[:, g], ACT.Copy
                                             ).then_inc(split_hi, 1)

            for half_ in range(2):
                act.wait_ge(ln_dve, half_ + 1)
                nc.scalar.activation(sq[:, 4 * half_:4 * half_ + 4, :],
                                     convb[:, 4 * half_:4 * half_ + 4, :], ACT.Square
                                     ).then_inc(ln_act, 1)
            ticks(G_OUT, RING, RING + 4)
            for c in range(CT):
                if c % 4 == 0:
                    act.wait_ge(ln_dve, 6 + c // 4)
                nc.scalar.activation(yb[:, c, :], convb[:, c, :], ACT.Silu,
                                     scale=cols[:, G_LNG + c:G_LNG + c + 1],
                                     bias=cols[:, G_LNB + c:G_LNB + c + 1]).then_inc(ln_act, 1)
                if c % 2:
                    act.wait_ge(ln_act, 2 + c + 1)
                    nc.scalar.activation(b_hi[:, CT + c - 1:CT + c + 1, :], yb[:, c - 1:c + 1, :],
                                         ACT.Copy).then_inc(split_hi, 1)

            for j in range(NCH):
                ticks(G_OUT + j * SPU, RING + (4 if j == 0 else 0), RING + SPU)
                if j < 2:
                    act.wait_ge(ya, 4)
                else:
                    act.wait_ge(ev_read, j - 1)
                evacuate(U_OUT + j, G_OUT + (j + 1) * SPU, ev[:, j % 2])
                act.wait_ge(evacuated, U_OUT + j + 1)
                squares(1, j, ev[:, j % 2], 8 + 2 * j)

            def residual(n, turned0, gain0, before):
                for c in range(NCH):
                    split(turned0 + 2 * c, a_hi, 4 * c, gain0)
                for c in range(NCH):
                    squares(n, c, h[:, :, c], before + 2 * c)

            residual(2, T_N1, G_MLPPRE, 16)

            with act.Fori(0, FF1 // D) as b:
                g, u = G_MLP + b * (2 * NCH * SPU), U_MLP + b * (2 * NCH)
                for j in range(NCH):
                    ticks(g, RING + j * SPU, RING + (j + 1) * SPU)
                    act.wait_ge(rs_ok, 3)
                    act.wait_ge(z_ready, b * NCH + (4 + j))
                    act.wait_ge(ev_read, b * NCH + 4)
                    evacuate((u, j % 2), g + (j + 1) * SPU, ev[:, j % 2], 2)
                    split(T_MLP + b * (2 * NCH) + 2 * j, b_hi, 4 * j)
                for j in range(NCH):
                    ticks(g, RING + (NCH + j) * SPU, RING + (NCH + j + 1) * SPU)
                    act.wait_ge(z_ready, b * NCH + 8)
                    act.wait_ge(ev_read, b * NCH + (4 + j))
                    evacuate((u, j % 2), g + (NCH + j + 1) * SPU, ev[:, j % 2])
                    act.wait_ge(ev_read, b * NCH + (4 + j + 1))
                    squares(3, j, wide[:, :, j], b * (2 * NCH) + (24 + 2 * j))
            residual(4, T_N2, G_MIX2, 56)

            with act.Fori(0, NCH) as i:
                for p_ in range(2):
                    g = G_QK + i * (2 * SPU) + p_ * SPU
                    ticks(g, RING, RING + SPU)
                    act.wait_ge(rs_ok, 5)
                    act.wait_ge(z_ready, i * 2 + (20 + p_))
                    evacuate((0, p_), g + SPU, ev[:, p_], 4)
                    for q in range(2):
                        act.wait_ge(turned, T_QK + 2 * p_ + q + 1 + i * 4)
                        for k in range(2):
                            head = i * 8 + (4 * p_ + 2 * q + k)
                            a_ = nc.scalar.activation(
                                qkT[:, bass.ds(head, 1), :].rearrange("p k s -> p (k s)"),
                                tp[:, q, k * S:(k + 1) * S], ACT.Copy, scale=qkg[:, bass.ds(head, 1)])
                        a_.then_inc(took, 1)

            def attend(n):
                if 1 <= n <= H_STICK:
                    act.wait_ge(att_dve, att_dve_at["sum", n - 1])
                    nc.scalar.activation(x0[:, :], x0[:, :], ACT.Exp).then_inc(att_act, 1)
                elif H_STICK < n <= NH:
                    act.wait_ge(turned, T_ATT + n)
                    act.wait_ge(valued, n - 1)
                    nc.scalar.activation(pT[:, :], tp[:, (n - 1) % 2, 0:3 * P], ACT.Copy
                                         ).then_inc(took, 1)
                if n >= 2:
                    act.wait_ge(valued, n - 1)
                    nc.scalar.activation(b_hi[:, n - 2, :], po[:, 0:S], ACT.Copy).then_inc(split_hi, 1)
                if n < H_STICK:
                    act.wait_ge(scored, n + 1)
                    if n:
                        act.wait_ge(att_dve, att_dve_at["weight", n - 1])
                    nc.scalar.activation(x0[:, :], sc[:, 0:3 * P], ACT.Abs, scale=QSCALE
                                         ).then_inc(att_act, 1)
                    act.wait_ge(att_act, att_act_at["abs", n])
                    nc.scalar.activation(x0[:, :], x0[:, :], ACT.Exp, scale=-1.0).then_inc(att_act, 1)
                    act.wait_ge(att_act, att_act_at["exp", n])
                    nc.scalar.activation(x0[:, :], x0[:, :], ACT.Ln, bias=1.0).then_inc(att_act, 1)
                elif n < NH:
                    act.wait_ge(att_dve, att_dve_at["neg", n])
                    for i, (a_, b_) in enumerate(((0, S), (S, 3 * P))):
                        own = n < H_STICK + H_BLOCK
                        e_ = nc.scalar.activation(x1[:, a_:b_], x0[:, a_:b_], ACT.Exp,
                                                  bias=nmx[:, i:i + 1],
                                                  accum_out=den[:, i:i + 1] if own else None)
                    e_.then_inc(att_act, 1)

            for u in range(U_V, U_B0):
                g = G_V + (u - U_V) * SPU
                for s in range(SPU):
                    ticks(g, RING + s, RING + s + 1)
                    for n in att_points(u, s):
                        attend(n)
                j = u - U_V
                if j < NCH:
                    evacuate(u, g + SPU, vv[:, :, j * W:(j + 1) * W], 4)
                else:
                    evacuate(u, g + SPU, gate[:, j - NCH], 4)

            def merge(g, u, mstep0, z0, pair0):
                s0 = 0
                for b, n in enumerate(BR_SLOTS):
                    ticks(g, RING + s0, RING + s0 + n)
                    s0 += n
                    act.wait_ge(z_ready, z0)
                    if b == 2:
                        act.wait_ge(mstep, mstep0 + 1)
                    p_ = (pair0 + b) % 2
                    evacuate((u, p_), g + s0, ev[:, p_])

            for b in range(3):
                act.wait_ge(evacuated, U_B0)
                nc.scalar.activation(gate[:, b], gate[:, b], ACT.Sigmoid).then_inc(gated, 1)
            merge(G_B0, U_B0, 0, 28, U_B0 % 2)
            with act.Fori(1, NCH) as j:
                g = G_J - 4 * SPU + j * (4 * SPU)
                for b in range(3):
                    ticks(g, RING + b * SPU, RING + b * SPU + 2)
                    if b == 0:
                        split(T_M - 2 + j * 2, m_hi, j * 4 - 4)
                    ticks(g, RING + b * SPU + 2, RING + (b + 1) * SPU)
                    act.wait_ge(z_ready, j + 28)
                    evacuate((0, b % 2), g + (b + 1) * SPU, gate[:, b], 4, ACT.Sigmoid)
                merge(g + 3 * SPU, 0, j * 4, j + 28, 1)

            for j in range(NCH):
                g = G_OUT2 + j * SPU
                ticks(g, RING, RING + 2)
                if j == 0:
                    split(T_M + 6, m_hi, 12)
                ticks(g, RING + 2, RING + SPU)
                act.wait_ge(z_ready, 32)
                if j > 1:
                    act.wait_ge(h_ready, 2 * NCH + j - 1)
                evacuate(U_OUT2 + j, g + SPU, ev[:, j % 2])
                split(T_N3 + 2 * j, a_hi, 4 * j, G_FFN2)
                squares(5, j, h[:, :, j], 64 + 2 * j)

            def ff_block(g, b, pairs, down_slots, last):
                z, r, tr = 32 + b * NCH, 4 + 16 + b * NCH, T_FF + b * (2 * NCH)
                for j in range(2 * pairs):
                    ticks(g, RING + j * SPU, RING + (j + 1) * SPU)
                    act.wait_ge(rs_ok, 6)
                    if j % 2 == 0:
                        act.wait_ge(z_ready, z + j // 2)
                        act.wait_ge(ev_read, r)
                    evacuate((0, j % 2), g + (j + 1) * SPU, ev[:, j % 2], 5,
                             ACT.Copy if j % 2 else ACT.Silu)
                    if j % 2:
                        split(tr + (j - 1), b_hi, 2 * (j - 1))
                s0 = 2 * pairs * SPU
                for j in range(NCH):
                    hi_ = RING + s0 + down_slots - (RING if last and j == NCH - 1 else 0)
                    ticks(g, RING + s0, hi_)
                    s0 += down_slots
                    act.wait_ge(z_ready, z + pairs)
                    if j > 1:
                        if last:
                            act.wait_ge(h_ready, 3 * NCH + j - 1)
                        else:
                            act.wait_ge(ev_read, r + (j - 1))
                    evacuate((0, j % 2), g + s0, ev[:, j % 2])

            with act.Fori(0, 2) as b:
                ff_block(G_FF + b * (3 * NCH * SPU), b, NCH, SPU, False)
            ff_block(G_FF3, 2, 3, 6, True)
        @block.vector
        def _(dve):
            def tick(g0, s, ring0=0):
                ring = (ring0 + s) % RING
                dve.wait_ge(hi_ready, g0 + (s + 1))
                nc.vector.tensor_tensor(w_lo[:, ring], raw[:, ring], w_hi[:, ring].bitcast(F32),
                                        ALU.subtract).then_inc(lo_ready, 1)

            def ticks(g0, s_from, s_to):
                for s in range(s_from, s_to):
                    tick(g0, s)

            def split(split0, hi, lo, k0, gain0=None):
                for g in range(2):
                    dve.wait_ge(split_hi, split0 + (g + 1))
                    if gain0 is None:
                        hi_, lo_ = (x[:, bass.ds(k0 + 2 * g, 2), :].rearrange("p k s -> p (k s)")
                                    for x in (hi, lo))
                        nc.vector.tensor_tensor(lo_, tp[:, g, :], hi_.bitcast(F32), ALU.subtract
                                                ).then_inc(split_lo, 1)
                        continue
                    for k in range(2):
                        kt = k0 + 2 * g + k
                        v = nc.vector.scalar_tensor_tensor(
                            lo[:, kt, :], tp[:, g, k * S:(k + 1) * S],
                            cols[:, gain0 + kt:gain0 + kt + 1], hi[:, kt, :].bitcast(F32),
                            ALU.mult, ALU.subtract)
                    v.then_inc(split_lo, 1)

            def mean_square(n, count):
                dve.wait_ge(squared, count)
                nc.vector.reduce_sum(ms[:, n, :], ssq[:, n], AX.X).then_inc(ssum, 1)
                dve.wait_ge(ssum, 2 * n + 1)
                nc.vector.tensor_scalar(ms[:, n, :], ms[:, n, :], 1.0 / D, EPS, ALU.mult, ALU.add
                                        ).then_inc(ssum, 1)

            nc.vector.memset(qkg[:, :], 1.0).then_inc(step0, 1)
            dve.wait_ge(cols_T, 1)
            nc.vector.tensor_copy(cols[:, :], sc[:, 0:3 * P]).then_inc(cols_ok, 1)
            dve.wait_ge(cols_ok, 1)
            dve.wait_ge(step0, 1)
            nc.vector.tensor_copy(qkg[:, H_STICK:NH], cols[:, G_QG:G_QG + H_SOFT]).then_inc(step0, 1)
            nc.vector.tensor_copy(qkg[:, NH + H_STICK:2 * NH], cols[:, G_KG:G_KG + H_SOFT]
                                  ).then_inc(step0, 1)

            for c in range(NCH):
                split(S_X + 2 * c, a_hi, a_lo, 4 * c, G_MIXPRE)
                ticks(G_IN, 2 * c, 2 * c + 2)
            mean_square(0, 8)

            def taps_long():
                n = 0
                for half_ in range(2):
                    for k in range(K_B):
                        for c in range(4 * half_, 4 * half_ + 4):
                            if k == 0 and c % 4 == 0:
                                dve.wait_ge(took, 4 * half_ // 2 + 2)
                            if k:
                                dve.wait_ge(conv, n - 3)
                            src = gT[:, c, k:k + S]
                            w_ = cols[:, G_CONVB + CT * k + c:G_CONVB + CT * k + c + 1]
                            if k == 0:
                                nc.vector.tensor_scalar(convb[:, c, :], src, w_,
                                                        cols[:, G_CBIAS + c:G_CBIAS + c + 1],
                                                        ALU.mult, ALU.add).then_inc(conv, 1)
                            else:
                                nc.vector.scalar_tensor_tensor(convb[:, c, :], src, w_,
                                                               convb[:, c, :], ALU.mult, ALU.add
                                                               ).then_inc(conv, 1)
                            n += 1
                            yield

            def taps_short():
                n = 0
                for half_ in range(2):
                    for k in range(K_A):
                        for c in range(4 * half_, 4 * half_ + 4):
                            if k == 0 and c % 4 == 0:
                                dve.wait_ge(took, 4 + 2 * half_ + 2)
                                if c == 0:
                                    dve.wait_ge(line_out, 32)
                            if k:
                                dve.wait_ge(conv3, n - 3)
                            src = cvT[:, c, k:k + S]
                            w_ = cols[:, G_CONVA + CT * k + c:G_CONVA + CT * k + c + 1]
                            if k == 0:
                                nc.vector.tensor_scalar(conva[:, c, :], src, w_, None, ALU.mult
                                                        ).then_inc(conv3, 1)
                            else:
                                nc.vector.scalar_tensor_tensor(conva[:, c, :], src, w_,
                                                               conva[:, c, :], ALU.mult, ALU.add
                                                               ).then_inc(conv3, 1)
                            n += 1
                            yield

            long_, short = taps_long(), taps_short()

            for u in range(10):
                for s in range(0 if u else RING, SPU):
                    tick(G_IN + u * SPU, RING + s)
                    if u >= 2:
                        for _ in range(4):
                            next(long_, None)
                    if u >= 7:
                        next(short, None)
                if u == 0:
                    dve.wait_ge(cols_T, 2)
                    nc.vector.tensor_tensor(line[:, :], po[0:H_SOFT, 0:LINE], lmask[:, :], ALU.add
                                            ).then_inc(cols_ok, 1)
                if u % 2 and u < 8:
                    dve.wait_ge(evacuated, u + 1)
                    if u > 1:
                        dve.wait_ge(turned, T_IN + u - 1)
                    nc.vector.tensor_tensor(zz[:, :, :], ev[:, 0], ev[:, 1], ALU.mult
                                            ).then_inc(z_ready, 1)
                if u >= 8:
                    for g in range(2):
                        dve.wait_ge(turned, T_IN + u + (u - 8) + g + 1)
                        c0 = 4 * (u - 8) + 2 * g
                        if g == 0:
                            dve.wait_ge(conv3, K_A * 4 * (u - 7))
                        if u == 9:
                            dve.wait_ge(split_lo, S_YA + g + 1)
                        nc.vector.tensor_tensor(
                            yt[:, g], tp[:, g, :].rearrange("p (c s) -> p c s", c=2),
                            conva[:, c0:c0 + 2, :], ALU.mult).then_inc(ya, 1)
                    for g in range(2):
                        c0 = 4 * (u - 8) + 2 * g
                        dve.wait_ge(split_hi, S_YA + 2 * (u - 8) + g + 1)
                        nc.vector.tensor_tensor(b_lo[:, c0:c0 + 2, :], yt[:, g],
                                                b_hi[:, c0:c0 + 2, :].bitcast(F32), ALU.subtract
                                                ).then_inc(split_lo, 1)
            for _ in long_:
                pass

            def over_channels(half_, row, op):
                part = convb[:, 4 * half_:4 * half_ + 4, :]
                return nc.vector.tensor_tensor(part, part, row.unsqueeze(1).to_broadcast([P, 4, S]), op)

            dve.wait_ge(ln_pe, 1)
            for half_ in range(2):
                over_channels(half_, sc[:, 0:S], ALU.subtract).then_inc(ln_dve, 1)
            ticks(G_OUT, RING, RING + 2)
            dve.wait_ge(ln_pe, 2)
            nc.vector.tensor_scalar(lnv[:, :], po[:, 0:TT], EPS, None, ALU.add).then_inc(ln_dve, 1)
            dve.wait_ge(ln_pool, 1)
            for tk in range(TT):
                nc.vector.tensor_scalar(dg[:, tk, :], ident[:, :], lnr[:, tk:tk + 1], None, ALU.mult
                                        ).then_inc(ln_dve, 1)
            dve.wait_ge(ln_pe, 3)
            for half_ in range(2):
                over_channels(half_, sc[:, S:2 * S], ALU.mult).then_inc(ln_dve, 1)
            ticks(G_OUT, RING + 2, RING + 4)
            for c in range(0, CT, 2):
                dve.wait_ge(split_hi, S_YB + c // 2 + 1)
                nc.vector.tensor_tensor(b_lo[:, CT + c:CT + c + 2, :], yb[:, c:c + 2, :],
                                        b_hi[:, CT + c:CT + c + 2, :].bitcast(F32), ALU.subtract
                                        ).then_inc(split_lo, 1)

            dve.wait_ge(gain1_in, 16)
            for j in range(NCH):
                ticks(G_OUT + j * SPU, RING + (4 if j == 0 else 0), RING + SPU)
                dve.wait_ge(evacuated, U_OUT + j + 1)
                row = gain[:, j * W:(j + 1) * W].unsqueeze(1).to_broadcast([P, TT, W])
                nc.vector.tensor_tensor(wide[:, :, j], ev[:, j % 2], row, ALU.mult
                                        ).then_inc(ev_read, 1)

            def residual(n, done, turned0, split0, gain0, scale_wide):
                def scaled(c):
                    row = gain[:, c * W:(c + 1) * W].unsqueeze(1).to_broadcast([P, TT, W])
                    nc.vector.tensor_tensor(wide[:, :, c], wide[:, :, c], row, ALU.mult
                                            ).then_inc(qstep, 1)

                if scale_wide:
                    scaled(0)
                dve.wait_ge(rs_ok, n + 1)
                for c in range(NCH):
                    if scale_wide:
                        dve.wait_ge(qstep, c + 1)
                    for tk in range(TT):
                        v = nc.vector.scalar_tensor_tensor(h[:, tk, c], wide[:, tk, c],
                                                           rs[:, n, tk:tk + 1], h[:, tk, c],
                                                           ALU.mult, ALU.add)
                    v.then_inc(h_ready, 1)
                    if scale_wide and c < NCH - 1:
                        scaled(c + 1)
                    split(split0 + 2 * c, a_hi, a_lo, 4 * c, gain0)

            mean_square(1, 16)
            dve.wait_ge(ev_read, NCH)
            residual(1, 0, T_N1, S_N1, G_MLPPRE, False)
            mean_square(2, 24)

            dve.wait_ge(wide_zero, 1)
            with dve.Fori(0, FF1 // D) as b:
                g, u = G_MLP + b * (2 * NCH * SPU), U_MLP + b * (2 * NCH)
                for j in range(NCH):
                    ticks(g, RING + j * SPU, RING + (j + 1) * SPU)
                    dve.wait_ge(evacuated, u + (j + 1))
                    dve.wait_ge(turned, T_MLP + b * (2 * NCH) + 2 * j)
                    nc.vector.scalar_tensor_tensor(zz[:, :, :], ev[:, j % 2], 0.0, ev[:, j % 2],
                                                   ALU.max, ALU.mult).then_inc(z_ready, 1)
                    split(S_MLP + b * (2 * NCH) + 2 * j, b_hi, b_lo, 4 * j)
                for j in range(NCH):
                    ticks(g, RING + (NCH + j) * SPU, RING + (NCH + j + 1) * SPU)
                    dve.wait_ge(evacuated, u + (NCH + j + 1))
                    dve.wait_ge(squared, b * (2 * NCH) + (18 + 2 * j))
                    nc.vector.tensor_tensor(wide[:, :, j], wide[:, :, j], ev[:, j % 2], ALU.add
                                            ).then_inc(ev_read, 1)
            mean_square(3, 56)
            dve.wait_ge(gain2_in, 16)
            residual(3, 4, T_N2, S_N2, G_MIX2, True)
            mean_square(4, 64)

            with dve.Fori(0, NCH) as i:
                for p_ in range(2):
                    ticks(G_QK + i * (2 * SPU) + p_ * SPU, RING, RING + SPU)
                    dve.wait_ge(evacuated, U_QK + p_ + 1 + i * 2)
                    dve.wait_ge(turned, T_QK + 2 * p_ + i * 4)
                    heads = zz.rearrange("p t (g d) -> p (t g) d", d=P)
                    v0 = i * 6 + (NCH + 3 * p_)
                    nc.vector.tensor_tensor(zz[:, :, :], ev[:, p_], ev[:, p_], ALU.mult
                                            ).then_inc(qstep, 1)
                    dve.wait_ge(qstep, v0 + 1)
                    nc.vector.reduce_sum(qss[:, :], heads, AX.X).then_inc(qstep, 1)
                    dve.wait_ge(qstep, v0 + 2)
                    nc.vector.tensor_scalar(qms[:, :], qss[:, :], 1.0 / P, EPS, ALU.mult, ALU.add
                                            ).then_inc(qstep, 1)
                    dve.wait_ge(qpool, i * 2 + (p_ + 1))
                    nc.vector.tensor_tensor(heads, ev[:, p_].rearrange("p t (g d) -> p (t g) d", d=P),
                                            qrs[:, :].unsqueeze(2).to_broadcast([P, 8, P]), ALU.mult
                                            ).then_inc(z_ready, 1)

            def attend(n):
                def step(v):
                    v.then_inc(att_dve, 1)

                def behind(stage, m):
                    dve.wait_ge(att_dve, att_dve_at[stage, m])

                parts = ((0, S), (S, 3 * P))
                if n == 0:
                    dve.wait_ge(consts_in, 48)
                if 1 <= n <= H_STICK:
                    dve.wait_ge(turned, T_ATT + n)
                    step(nc.vector.tensor_tensor(x0[:, :], x1[:, :], tp[:, (n - 1) % 2, 0:3 * P],
                                                 ALU.add))
                if n >= 2:
                    dve.wait_ge(split_hi, S_O + n - 1)
                    nc.vector.tensor_tensor(b_lo[:, n - 2, :], po[:, 0:S],
                                            b_hi[:, n - 2, :].bitcast(F32), ALU.subtract
                                            ).then_inc(split_lo, 1)
                if 1 <= n <= H_STICK:
                    dve.wait_ge(att_act, att_act_at["weight", n - 1])
                    if n > 1:
                        dve.wait_ge(valued, n - 1)
                    for a_, b_ in parts:
                        step(nc.vector.tensor_tensor(pT[:, a_:b_], x0[:, a_:b_], past[:, 0:b_ - a_],
                                                     ALU.mult))
                if n < H_STICK:
                    dve.wait_ge(scored, n + 1)
                    dve.wait_ge(att_act, att_act_at["log", n])
                    step(nc.vector.tensor_scalar(x1[:, :], sc[:, 0:3 * P], QSCALE, 0.0, ALU.mult,
                                                 ALU.min))
                    behind("min", n)
                    step(nc.vector.tensor_tensor(x1[:, :], x1[:, :], x0[:, :], ALU.subtract))
                    behind("logb", n)
                    step(nc.vector.scalar_tensor_tensor(x2[:, :], sc[:, 0:3 * P], -QSCALE, x1[:, :],
                                                        ALU.mult, ALU.add))
                    behind("log1", n)
                    for a_, b_ in parts:
                        step(nc.vector.tensor_tensor(x2[:, a_:b_], x2[:, a_:b_], past[:, 0:b_ - a_],
                                                     ALU.mult))
                elif n < NH:
                    m = n - H_STICK
                    bias_ = bias[:, m % 2, :]
                    if n == H_STICK:
                        behind("weight", n - 1)
                    dve.wait_ge(scored, n + 1)
                    dve.wait_ge(bias_in[m % 2], 16 * (m // 2 + 1))
                    for (a_, b_), tab in zip(parts, (bias_, bias_[:, P:S])):
                        step(nc.vector.scalar_tensor_tensor(x0[:, a_:b_], sc[:, a_:b_], QSCALE, tab,
                                                            ALU.mult, ALU.add))
                    behind("logits", n)
                    for i, (a_, b_) in enumerate(parts):
                        step(nc.vector.reduce_max(mx[:, i:i + 1], x0[:, a_:b_], AX.X))
                    behind("max", n)
                    step(nc.vector.tensor_scalar(nmx[:, :], mx[:, :], -1.0, None, ALU.mult))
                    dve.wait_ge(att_act, att_act_at["exp", n])
                    if m >= H_BLOCK:
                        for i, (a_, b_) in enumerate(parts):
                            step(nc.vector.scalar_tensor_tensor(
                                x1[:, a_:b_], x1[:, a_:b_], 1.0, cnt[:, a_:b_], ALU.mult, ALU.mult,
                                accum_out=den[:, i:i + 1]))
                        behind("count", n)
                    step(nc.vector.reciprocal(rden[:, :], den[:, :]))
                    behind("recip", n)
                    dve.wait_ge(turned, T_ATT + n)
                    for i, (a_, b_) in enumerate(parts):
                        step(nc.vector.tensor_scalar(x2[:, a_:b_], x1[:, a_:b_], rden[:, i:i + 1],
                                                     None, ALU.mult))

            for u in range(U_V, U_B0):
                for s in range(SPU):
                    tick(G_V + (u - U_V) * SPU, RING + s)
                    for n in att_points(u, s):
                        attend(n)

            def merge(g, u, mstep0, pair0):
                s0 = 0
                for b, n in enumerate(BR_SLOTS):
                    ticks(g, RING + s0, RING + s0 + n)
                    s0 += n
                    e_ = ev[:, (pair0 + b) % 2]
                    dve.wait_ge(evacuated, u + (b + 1))
                    if b == 0:
                        nc.vector.tensor_tensor(zz[:, :, :], gate[:, b], e_, ALU.mult
                                                ).then_inc(mstep, 1)
                        continue
                    nc.vector.tensor_tensor(e_, gate[:, b], e_, ALU.mult).then_inc(mstep, 1)
                    dve.wait_ge(mstep, mstep0 + 2 * b)
                    v = nc.vector.tensor_tensor(zz[:, :, :], zz[:, :, :], e_, ALU.add)
                    v.then_inc(*((z_ready, 1) if b == 2 else (mstep, 1)))

            dve.wait_ge(gated, 3)
            merge(G_B0, U_B0, 0, U_B0 % 2)
            with dve.Fori(1, NCH) as j:
                g, u = G_J - 4 * SPU + j * (4 * SPU), U_J - 6 + j * 6
                for b in range(3):
                    ticks(g, RING + b * SPU, RING + b * SPU + 2)
                    if b == 0:
                        split(S_M - 2 + j * 2, m_hi, m_lo, j * 4 - 4)
                    ticks(g, RING + b * SPU + 2, RING + (b + 1) * SPU)
                merge(g + 3 * SPU, u + 3, j * 4, 1)

            for j in range(NCH):
                g = G_OUT2 + j * SPU
                ticks(g, RING, RING + 2)
                if j == 0:
                    split(S_M + 6, m_hi, m_lo, 12)
                ticks(g, RING + 2, RING + SPU)
                dve.wait_ge(evacuated, U_OUT2 + j + 1)
                nc.vector.tensor_tensor(h[:, :, j], h[:, :, j], ev[:, j % 2], ALU.add
                                        ).then_inc(h_ready, 1)
                split(S_N3 + 2 * j, a_hi, a_lo, 4 * j, G_FFN2)
            mean_square(5, 72)

            def ff_block(g, u, b, pairs, down_slots, last):
                for j in range(2 * pairs):
                    ticks(g, RING + j * SPU, RING + (j + 1) * SPU)
                    if j % 2 == 0:
                        continue
                    dve.wait_ge(evacuated, u + (j + 1))
                    dve.wait_ge(turned, T_FF + b * (2 * NCH) + (j - 1))
                    nc.vector.tensor_tensor(zz[:, :, :], ev[:, 0], ev[:, 1], ALU.mult
                                            ).then_inc(z_ready, 1)
                    split(S_FF + b * (2 * NCH) + (j - 1), b_hi, b_lo, 2 * (j - 1))
                    if last and j == 1:
                        for c in range(NCH):
                            nc.vector.tensor_tensor(h[:, :, c], h[:, :, c], wide[:, :, c], ALU.add
                                                    ).then_inc(folded, 1)
                s0 = 2 * pairs * SPU
                for j in range(NCH):
                    ticks(g, RING + s0,
                          RING + s0 + down_slots - (RING if last and j == NCH - 1 else 0))
                    s0 += down_slots
                    dve.wait_ge(evacuated, u + (2 * pairs + j + 1))
                    if last:
                        dve.wait_ge(folded, j + 1)
                        nc.vector.tensor_tensor(h[:, :, j], h[:, :, j], ev[:, j % 2], ALU.add
                                                ).then_inc(h_ready, 1)
                    else:
                        nc.vector.tensor_tensor(wide[:, :, j], wide[:, :, j], ev[:, j % 2], ALU.add
                                                ).then_inc(ev_read, 1)

            dve.wait_ge(wide_zero, 2)
            with dve.Fori(0, 2) as b:
                ff_block(G_FF + b * (3 * NCH * SPU), U_FF + b * (3 * NCH), b, NCH, SPU, False)
            ff_block(G_FF3, U_FF + 6 * NCH, 2, 3, 6, True)

        @block.gpsimd
        def _(pool):
            nc.gpsimd.memset(mean_w[:, :], 1.0 / D_A)
            nc.gpsimd.memset(ones[:, :], 1.0)
            nc.gpsimd.memset(half[:, :], -0.5)
            nc.gpsimd.memset(qexp[:, :, :], -0.5)
            nc.gpsimd.memset(gT[:, :, 0:K_B - 1], 0.0)
            nc.gpsimd.memset(cvT[:, :, 0:K_A - 1], 0.0).then_inc(const_set, 1)
            pool.wait_ge(const_set, 1)
            nc.gpsimd.memset(qexp[:, 0:8:4, :], 0.0).then_inc(const_set, 1)
            pool.dma_start(gain[:, :], bass.AP(t["mix_post_gain"].tensor, 0, [[0, P], [1, D]])
                           ).then_inc(gain1_in, 16)
            pool.wait_ge(cols_ok, 2)
            pool.dma_start(line_dram, line[:, :]).then_inc(line_out, 16)
            pool.wait_ge(line_out, 16)
            pool.dma_start(t["skew_dram"], line_dram.unsqueeze(1).to_broadcast([H_SOFT, P, LINE])
                           ).then_inc(line_out, 16)

            def root(n):
                pool.wait_ge(ssum, 2 * n + 2)
                nc.gpsimd.tensor_tensor(rs[:, n, :], ms[:, n, :], half[:, :], ALU.pow
                                        ).then_inc(rs_ok, 1)

            root(0)
            pool.wait_ge(ln_dve, 3)
            nc.gpsimd.tensor_tensor(lnr[:, :], lnv[:, :], half[:, :], ALU.pow).then_inc(ln_pool, 1)
            root(1)
            pool.wait_ge(h_ready, NCH)
            nc.gpsimd.memset(wide[:, :, :, :], 0.0).then_inc(wide_zero, 1)
            pool.dma_start(gain[:, :], bass.AP(t["mlp_post_gain"].tensor, 0, [[0, P], [1, D]])
                           ).then_inc(gain2_in, 16)
            root(2)
            root(3)
            root(4)
            with pool.Fori(0, NCH) as i:
                for p_ in range(2):
                    pool.wait_ge(qstep, i * 6 + (NCH + 3 * p_ + 3))
                    nc.gpsimd.tensor_tensor(
                        qrs[:, :], qms[:, :],
                        qexp[:, bass.ds(i * 2 + p_, 1), :].rearrange("p u g -> p (u g)"),
                        ALU.pow).then_inc(qpool, 1)

            pool.wait_ge(turned, T_ATT)
            pool.dma_start(cnt[:, :], t["cnt"]).then_inc(consts_in, 16)
            pool.dma_start(past[:, :], t["past"]).then_inc(consts_in, 16)
            pool.dma_start(tri[:, :], t["tri"]).then_inc(consts_in, 16)
            pool.wait_ge(line_out, 32)
            for m in range(H_SOFT):
                if m >= 2:
                    pool.wait_ge(att_dve, att_dve_at["logits", H_STICK + m - 2])
                src = bass.AP(t["skew_dram"].tensor, m * P * LINE + P - 1, [[LINE - 1, P], [1, S]])
                pool.dma_start(bias[:, m % 2, :], src).then_inc(bias_in[m % 2], 16)
            pool.wait_ge(evacuated, U_B0 + 1)
            nc.gpsimd.memset(wide[:, :, :, :], 0.0).then_inc(wide_zero, 1)
            root(5)


def tables():
    dist = 255 - np.arange(LINE)
    d = np.maximum(dist, 1).astype(np.float64)
    far = np.minimum(16 + np.floor(np.log(d / 16) / np.log(2048 / 16) * 16).astype(np.int64), 31)
    bucket = np.where(dist < 16, np.maximum(dist, 0), far)
    onehot = (np.arange(32)[:, None] == bucket[None, :]).astype(np.float32)

    def patterns(x):
        return ((x >= 0) * 1 * (x <= 128) + ((x >= 0) & (x % 4 == 0)) + ((x >= 0) & (x % 16 == 0)))

    lmask = np.zeros((H_SOFT, LINE), np.float32)
    lmask[:H_BLOCK, dist < 0] = -1e30
    lmask[H_BLOCK:, patterns(dist) == 0] = -1e30
    p = np.arange(P)[:, None]
    cnt = np.concatenate([patterns(P + p - np.arange(S)[None]), patterns(p - np.arange(P)[None])], 1)
    return {"ident": np.eye(P, dtype=np.float32), "onehot": onehot, "lmask": lmask,
            "cnt": cnt.astype(np.float32), "past": (np.arange(S)[None] > p).astype(np.float32),
            "tri": (p > np.arange(P)[None]).astype(np.float32)}


NAMES = ["x", "mix_pre_gain", "w_in", "conv_a_w", "conv_b_w", "conv_b_bias", "ln_b_gain", "ln_b_bias",
         "w_out", "mix_post_gain", "mlp_pre_gain", "w_up", "w_down", "mlp_post_gain", "g_mix_2",
         "w_in_2", "q_gain_2", "k_gain_2", "w_branch_2", "w_out_2", "g_ffn_2", "w_gu_2", "w_down_2",
         "rel_bias_2"]


def kernel(**inputs):
    import concourse.bacc as bacc
    from concourse.bass_utils import run_bass_kernel_spmd

    nc = bacc.Bacc("TRN2", target_bir_lowering=False, num_devices=1)
    arrays, args = {}, {}
    for name, value in [(n, inputs[n]) for n in NAMES] + list(tables().items()):
        a = np.ascontiguousarray(value)
        arrays[name + "_dram"] = a
        args[name] = nc.dram_tensor(name + "_dram", a.shape, mybir.dt.from_np(a.dtype),
                                    kind="ExternalInput").ap()
    args["out"] = nc.dram_tensor("out_dram", (1, S, D), F32, kind="ExternalOutput").ap()
    args["line_dram"] = nc.dram_tensor("line_dram", (H_SOFT, LINE), F32, kind="Internal").ap()
    args["skew_dram"] = nc.dram_tensor("skew_dram", (H_SOFT, P, LINE), F32, kind="Internal").ap()
    build_program(nc, args)
    result = run_bass_kernel_spmd(nc, [arrays], core_ids=[0])
    return result.results[0]["out_dram"]
```

```python
from contextlib import ExitStack

import concourse.bass as bass
import numpy as np
from concourse import mybir

F32 = mybir.dt.float32
F32R = mybir.dt.float32r
ACT = mybir.ActivationFunctionType
ALU = mybir.AluOpType
AX = mybir.AxisListType

P = 128
D = 2048
S = 256
TT = S // P
W = 512
NCH = D // W
RING = 4
KS = 2
KT = D // P
SPU = KT // KS
EPS = 1e-6

D_A = D // 2
K_A, K_B = 3, 31
CT = D_A // P
POOL_TILES = (3, 7)
POOL_STEPS = 2 * K_B - 1
FF1 = 4 * D
FF2 = 5632
NH = 16
H_STICK, H_BLOCK, H_DIL = 4, 6, 6
H_SOFT = H_BLOCK + H_DIL
QSCALE = float(P) ** -0.5
SKEWS = 3
LINE = 384

G_MIXPRE, G_MLPPRE, G_MIX2, G_FFN2 = 0, 16, 32, 48
G_CBIAS, G_LNG, G_LNB, G_CONVA = 64, 72, 80, 88
G_CONVB = 112
G_QG, G_KG = 360, 372
ROWS = (112, 124, 124, 24)

U_IN, U_OUT, U_MLP, U_QK, U_V, U_G0, U_B0, U_J, U_OUT2, U_FF = 0, 10, 14, 46, 54, 58, 61, 64, 82, 86
G_IN, G_OUT, G_MLP, G_QK, G_V, G_G0, G_B0, G_J, G_OUT2, G_FF = 0, 80, 112, 368, 432, 464, 488, 496, 592, 624
G_FF3 = G_FF + 192
G_DN3 = G_FF3 + 48
G_END = G_DN3 + 24
T_X, T_IN, T_N1, T_MLP, T_N2, T_QK, T_ATT, T_M, T_N3, T_FF = 0, 8, 20, 28, 60, 68, 84, 100, 108, 116
S_X, S_YA, S_YB, S_N1, S_MLP, S_N2, S_O, S_M, S_N3, S_FF = 0, 8, 12, 16, 24, 56, 64, 80, 88, 96
K_QK, K_ATT = 8, 24
IN_COLS = [3 * D_A, 4 * D_A, 3 * D_A + W, 4 * D_A + W, D_A, 2 * D_A, D_A + W, 2 * D_A + W, 0, W]
ATT_SLOTS = (7, 11, 15, 18, 22, 25, 27, 30, 32, 35, 37, 39, 42, 44, 47, 49, 52, 54)
BR_SLOTS = (H_STICK // KS, H_BLOCK // KS, H_DIL // KS)


def build_program(nc, t):
    ctx = ExitStack()
    with ctx:
        base = -(-nc.sbuf_base // 32) * 32
        ctx.enter_context(nc.sbuf_tensor("arena", [P, 207 * 256], F32))

        def at(name, kb, shape, dt=F32):
            return nc.alloc_sbuf_tensor_at(name, shape, dt, offset=base + int(kb * 1024))

        def ps(name, shape):
            return ctx.enter_context(nc.psum_tensor(name, shape, F32))

        def sem(name):
            return ctx.enter_context(nc.semaphore(name))

        raw = at("raw", 0, [P, RING, KS, W])
        w_hi = at("w_hi", 16, [P, RING, KS, W], F32R)
        w_lo = at("w_lo", 32, [P, RING, KS, W], F32R)
        a_hi = at("a_hi", 48, [P, KT, S], F32R)
        a_lo = at("a_lo", 64, [P, KT, S], F32R)
        b_hi = at("b_hi", 80, [P, KT, S], F32R)
        b_lo = at("b_lo", 96, [P, KT, S], F32R)
        rows = at("rows", 112, [P, 4, P])
        onehot = at("onehot", 114, [32, LINE])
        lmask = at("lmask", 116, [H_SOFT, LINE])
        line = at("line", 118, [H_SOFT, LINE])
        relb = at("relb", 120, [32, H_SOFT])
        conva = at("conva", 112, [P, CT, S])
        yt = at("yt", 120, [P, 2, 2, S])
        prod = at("prod", 124, [P, 4, S])
        wide = at("wide", 112, [P, TT, NCH, W])
        vv = at("vv", 112, [P, TT, D])
        h = at("h", 128, [P, TT, NCH, W])
        gT = at("gT", 144, [P, CT, K_B - 1 + S])
        sq = at("sq", 144, [P, CT, S])
        cvT = at("cvT", 153.5, [P, CT, K_A - 1 + S])
        convb = at("convb", 162, [P, CT, S])
        dg = at("dg", 170, [P, TT, P])
        yb = at("yb", 153.5, [P, CT, S])
        qkT = at("qkT", 144, [P, 2 * NH, S])
        m_hi = at("m_hi", 144, [P, KT, S], F32R)
        m_lo = at("m_lo", 160, [P, KT, S], F32R)
        gain = at("gain", 176, [P, D])
        gate = at("gate", 176, [P, 3, TT, W])
        ev = at("ev", 188, [P, 2, TT, W])
        zz = at("zz", 196, [P, TT, W])
        bias = at("bias", 188, [P, 2, S])
        cnt = at("cnt", 190, [P, 3 * P])
        past = at("past", 191.5, [P, S])
        tri = at("tri", 192.5, [P, P])
        x0 = at("x0", 193, [P, 3 * P])
        x1 = at("x1", 194.5, [P, 3 * P])
        x2 = at("x2", 196, [P, 3 * P])
        pT = at("pT", 197.5, [P, 3 * P])
        ident = at("ident", 200, [P, P])
        mean_w = at("mean_w", 200.5, [P, P])
        ones = at("ones", 201, [P, P])
        cols = at("cols", 201.5, [P, 3 * P])
        junk = at("junk", 203, [P, TT, W], mybir.dt.bfloat16)
        ssq = at("ssq", 205, [P, 6, TT, NCH])
        rs = at("rs", 205.25, [P, 6, TT])
        ms = at("ms", 205.375, [P, 6, TT])
        half = at("half", 205.5, [P, TT])
        lnv = at("lnv", 205.53125, [P, TT])
        qkg = at("qkg", 206.125, [P, 2 * NH])
        lnr = at("lnr", 205.5625, [P, TT])
        qexp = at("qexp", 205.625, [P, 8, 8])
        qss = at("qss", 205.875, [P, 8])
        qms = at("qms", 205.90625, [P, 8])
        qrs = at("qrs", 205.9375, [P, 8])
        mx = at("mx", 206, [P, 2])
        den = at("den", 206.03125, [P, 2])
        rden = at("rden", 206.0625, [P, 2])
        nmx = at("nmx", 206.09375, [P, 2])

        acc = ps("acc", [P, 2, TT, W])
        tp = ps("tp", [P, 2, W])
        sc = ps("sc", [P, W])
        po = ps("po", [P, W])

        landed = [sem(f"landed{i}") for i in range(RING)]
        hi_ready = sem("hi_ready")
        lo_ready = sem("lo_ready")
        slot_used = sem("slot_used")
        evacuated = sem("evacuated")
        turned = sem("turned")
        split_hi = sem("split_hi")
        split_lo = sem("split_lo")
        took = sem("took")
        z_ready = sem("z_ready")
        ev_read = sem("ev_read")
        x_in = [sem(f"x_in{c}") for c in range(NCH)]
        ident_in = sem("ident_in")
        pre_in = sem("pre_in")
        rows_in = sem("rows_in")
        line_in = sem("line_in")
        gain1_in = sem("gain1_in")
        gain2_in = sem("gain2_in")
        line_out = sem("line_out")
        consts_in = sem("consts_in")
        bias_in = [sem("bias_in0"), sem("bias_in1")]
        out_stored = sem("out_stored")
        const_set = sem("const_set")
        cols_T = sem("cols_T")
        cols_ok = sem("cols_ok")
        squared = sem("squared")
        ssum = sem("ssum")
        rs_ok = sem("rs_ok")
        h_ready = sem("h_ready")
        step0 = sem("step0")
        conv = sem("conv")
        conv_pool = sem("conv_pool")
        conv3 = sem("conv3")
        ya = sem("ya")
        ln_pe = sem("ln_pe")
        ln_dve = sem("ln_dve")
        ln_act = sem("ln_act")
        ln_pool = sem("ln_pool")
        qstep = sem("qstep")
        qpool = sem("qpool")
        folded = sem("folded")
        mstep = sem("mstep")
        gated = sem("gated")
        scored = sem("scored")
        valued = sem("valued")
        att_dve = sem("att_dve")
        att_act = sem("att_act")
        wide_zero = sem("wide_zero")

        line_dram = t["line_dram"]
        w_in = t["w_in"][0].rearrange("(k p) n -> p k n", p=P)
        w_out = t["w_out"][0].rearrange("(k p) n -> p k n", p=P)
        w_up = t["w_up"][0].rearrange("(k p) n -> p k n", p=P)
        w_down = t["w_down"][0].rearrange("(k p) n -> p k n", p=P)
        w_in2 = t["w_in_2"][0].rearrange("(k p) n -> p k n", p=P)
        w_br = t["w_branch_2"][0].rearrange("(k p) n -> p k n", p=P)
        w_out2 = t["w_out_2"][0].rearrange("(k p) n -> p k n", p=P)
        w_gu = t["w_gu_2"][0].rearrange("(k p) n -> p k n", p=P)
        w_dn2 = t["w_down_2"][0].rearrange("(k p) n -> p k n", p=P)
        x_v = t["x"][0].rearrange("(t p) (c n) -> p t c n", p=P, n=W)
        out_v = t["out"][0].rearrange("(t p) (c n) -> p t c n", p=P, n=W)

        att_act_at, att_dve_at = {}, {}
        n_act = n_dve = 0
        for n in range(NH + 1):
            if 1 <= n <= H_STICK:
                n_act += 1
                att_act_at["weight", n - 1] = n_act
                att_dve_at["sum", n - 1] = n_dve + 1
                n_dve += 3
                att_dve_at["weight", n - 1] = n_dve
            if n < H_STICK:
                for stage in ("abs", "exp", "log"):
                    n_act += 1
                    att_act_at[stage, n] = n_act
                for stage, ops in (("min", 1), ("logb", 1), ("log1", 1), ("masked", 2)):
                    n_dve += ops
                    att_dve_at[stage, n] = n_dve
            elif n < NH:
                n_act += 1
                att_act_at["exp", n] = n_act
                counted = (("count", 2),) if n >= H_STICK + H_BLOCK else ()
                for stage, ops in (("logits", 2), ("max", 2), ("neg", 1), *counted, ("recip", 1),
                                   ("prob", 2)):
                    n_dve += ops
                    att_dve_at[stage, n] = n_dve

        def att_points(u, i):
            slot = (u - U_V) * SPU + i
            return [ATT_SLOTS.index(slot)] if slot in ATT_SLOTS else []

        def tap_weight(c, k):
            return cols[:, G_CONVB + CT * k + c:G_CONVB + CT * k + c + 1]

        def tap_first(engine, c):
            return engine.tensor_scalar(convb[:, c, :], gT[:, c, 0:S], tap_weight(c, 0),
                                        cols[:, G_CBIAS + c:G_CBIAS + c + 1], ALU.mult, ALU.add)

        block = ctx.enter_context(nc.Block())

        @block.sync
        def _(sp):
            def load(s, g, src):
                ring = s % RING
                if g is not None:
                    sp.wait_ge(lo_ready, g - RING + 1)
                sp.dma_start(raw[:, ring, 0:src.shape[1]], src).then_inc(landed[ring], 16)

            def ks(s):
                return slice(KS * s, KS * s + KS)

            sp.dma_start(ident[:, :], t["ident"]).then_inc(ident_in, 16)
            for c in range(NCH):
                sp.dma_start(h[:, :, c], x_v[:, :, c]).then_inc(x_in[c], 16)
                load(c, None, w_in[:, ks(c), IN_COLS[0]:IN_COLS[0] + W])
            small = ((16, "mlp_pre_gain", KT), (32, "g_mix_2", KT), (48, "g_ffn_2", KT),
                     (64, "conv_b_bias", CT), (72, "ln_b_gain", CT), (80, "ln_b_bias", CT),
                     (88, "conv_a_w", K_A * CT))
            for r0, name, n in small:
                src = t[name][0]
                src = (src.rearrange("(c p) -> c p", p=P) if len(src.shape) == 1
                       else src.rearrange("k (c p) -> (k c) p", p=P))
                sp.dma_start(rows[r0:r0 + n, 0, :], src).then_inc(rows_in, 16)
            taps = t["conv_b_w"][0].rearrange("k (c p) -> (k c) p", p=P)
            for i in range(2):
                sp.dma_start(rows[0:124, 1 + i, :], taps[124 * i:124 * (i + 1), :]).then_inc(rows_in, 16)
            sp.dma_start(rows[0:H_SOFT, 3, :], t["q_gain_2"][0]).then_inc(rows_in, 16)
            sp.dma_start(rows[H_SOFT:2 * H_SOFT, 3, :], t["k_gain_2"][0]).then_inc(rows_in, 16)
            sp.dma_start(onehot[:, :], t["onehot"]).then_inc(line_in, 16)
            sp.dma_start(lmask[:, :], t["lmask"]).then_inc(line_in, 16)
            sp.dma_start(relb[:, :], t["rel_bias_2"]).then_inc(line_in, 16)
            for u in range(10):
                for s in range(SPU):
                    g = G_IN + u * SPU + s
                    if g >= RING:
                        load(g, g, w_in[:, ks(s), IN_COLS[u]:IN_COLS[u] + W])
            with sp.Fori(0, NCH // 2) as j:
                src = w_out[:, :, bass.ds(sp.snap(j * (2 * W)), 2 * W)]
                for i in range(2 * SPU):
                    part, unit, s = i // SPU, i // RING % 2, i % RING
                    load(i, G_OUT + j * (2 * SPU) + i,
                         src[:, ks(part * RING + s), unit * W:(unit + 1) * W])
            with sp.Fori(0, FF1 // D) as b:
                g = G_MLP + b * (2 * NCH * SPU)
                up = w_up[:, :, bass.ds(sp.snap(b * D), D)]
                down = w_down[:, bass.ds(sp.snap(b * KT), KT)]
                for j in range(NCH):
                    for s in range(SPU):
                        load(s, g + (j * SPU + s), up[:, ks(s), j * W:(j + 1) * W])
                for j in range(NCH):
                    for s in range(SPU):
                        load(s, g + ((NCH + j) * SPU + s), down[:, ks(s), j * W:(j + 1) * W])
            with sp.Fori(0, 3 * NCH) as j:
                src = w_in2[:, :, bass.ds(sp.snap(j * W), W)]
                for s in range(SPU):
                    load(s, G_QK + j * SPU + s, src[:, ks(s)])
            for b in range(3):
                for s in range(SPU):
                    g = G_G0 + b * SPU + s
                    load(g, g, w_in2[:, ks(s), (3 + b) * D:(3 + b) * D + W])
            for s in range(SPU):
                load(s, G_B0 + s, w_br[:, ks(s), 0:W])
            with sp.Fori(1, NCH) as j:
                g = G_J - 4 * SPU + j * (4 * SPU)
                col = sp.snap((j - 1) * W)
                for b in range(3):
                    src = w_in2[:, :, (3 + b) * D + W:(4 + b) * D][:, :, bass.ds(col, W)]
                    for s in range(SPU):
                        load(s, g + (b * SPU + s), src[:, ks(s)])
                src = w_br[:, :, W:][:, :, bass.ds(col, W)]
                for s in range(SPU):
                    load(s, g + (3 * SPU + s), src[:, ks(s)])
            with sp.Fori(0, NCH) as j:
                src = w_out2[:, :, bass.ds(sp.snap(j * W), W)]
                for s in range(SPU):
                    load(s, G_OUT2 + j * SPU + s, src[:, ks(s)])
            with sp.Fori(0, 2) as b:
                g = G_FF + b * (3 * NCH * SPU)
                col = sp.snap(b * D)
                halves = [w_gu[:, :, i * FF2:(i + 1) * FF2][:, :, bass.ds(col, D)] for i in range(2)]
                down = w_dn2[:, bass.ds(sp.snap(b * KT), KT)]
                for j in range(2 * NCH):
                    for s in range(SPU):
                        c0 = (j // 2) * W
                        load(s, g + (j * SPU + s), halves[j % 2][:, ks(s), c0:c0 + W])
                for j in range(NCH):
                    for s in range(SPU):
                        load(s, g + ((2 * NCH + j) * SPU + s), down[:, ks(s), j * W:(j + 1) * W])
            for j in range(6):
                for s in range(SPU):
                    g = G_FF3 + j * SPU + s
                    c0 = 2 * D + (j // 2) * W + (j % 2) * FF2
                    load(g, g, w_gu[:, ks(s), c0:c0 + W])
            for j in range(NCH):
                for s in range(6):
                    g = G_DN3 + 6 * j + s
                    load(g, g, w_dn2[:, 2 * KT + KS * s:2 * KT + KS * s + KS, j * W:(j + 1) * W])
            for j in range(NCH):
                sp.wait_ge(h_ready, 3 * NCH + j + 1)
                sp.dma_start(out_v[:, :, j], h[:, :, j]).then_inc(out_stored, 16)
            sp.wait_ge(out_stored, 16 * NCH)

        @block.tensor
        def _(pe):
            def slots(g0, u, s_from, s_to, hi, lo, split0=None, n=SPU, k0=0, ring0=0, pair=0):
                if s_from == 0 and not (isinstance(u, int) and u < 2):
                    pe.wait_ge(evacuated, u - 1)
                for s in range(s_from, s_to):
                    if split0 is not None:
                        pe.wait_ge(split_lo, split0 + s + 1)
                    pe.wait_ge(lo_ready, g0 + (s + 1))
                    ring = (ring0 + s) % RING
                    for k in range(KS):
                        kt = k0 + KS * s + k
                        for tk in range(TT):
                            out = acc[:, pair, tk, :]
                            xh, xl = (part[:, kt, tk * P:(tk + 1) * P] for part in (hi, lo))
                            wh, wl = w_hi[:, ring, k, :], w_lo[:, ring, k, :]
                            nc.tensor.matmul(out, xh, wl, start=s == 0 and k == 0, stop=False)
                            nc.tensor.matmul(out, xh, wh, start=False, stop=False)
                            mm = nc.tensor.matmul(out, xl, wh, start=False,
                                                  stop=s == n - 1 and k == KS - 1)
                    mm.then_inc(slot_used, 1)

            def turn(src, need, free=None):
                pe.wait_ge(*need)
                for g in range(2):
                    if free is not None:
                        pe.wait_ge(free[0], free[1] + g)
                    for k in range(2):
                        for tk in range(TT):
                            c = (2 * g + k) * P
                            tr = nc.tensor.transpose(tp[:, g, (2 * k + tk) * P:(2 * k + tk + 1) * P],
                                                     src[:, tk, c:c + P], ident[:, :])
                    tr.then_inc(turned, 1)

            def turn_residual(g, u, need, split0):
                for c in range(NCH):
                    free = (split_lo, split0 + 2 * c - 1) if split0 + c else None
                    turn(h[:, :, c, :], need[c], free)
                    if c:
                        slots(g, u, 2 * c - 2, 2 * c, a_hi, a_lo, split0=split0)

            pe.wait_ge(ident_in, 16)
            pe.wait_ge(pre_in, 16)
            nc.tensor.transpose(sc[:, 0:KT], rows[0:KT, 0, :], ident[0:KT, 0:KT]).then_inc(cols_T, 1)
            turn_residual(G_IN, 0, [(x_in[c], 16) for c in range(NCH)], S_X)
            slots(G_IN, 0, SPU - 2, SPU, a_hi, a_lo, split0=S_X)
            pe.wait_ge(rows_in, 16 * 11)
            pe.wait_ge(cols_ok, 1)
            start = 0
            for i, n in enumerate(ROWS):
                tr = nc.tensor.transpose(sc[:, start:start + n], rows[0:n, i, :], ident[0:n, 0:n])
                start += n
            tr.then_inc(cols_T, 1)
            pe.wait_ge(line_in, 48)
            nc.tensor.matmul(po[0:H_SOFT, 0:LINE], relb[:, :], onehot[:, :], start=True,
                             stop=True).then_inc(cols_T, 1)

            def in_product(u):
                if u in (2, 4, 6, 8):
                    i = u // 2
                    turn(zz, (z_ready, i), (took, 2 * i - 3) if i > 1 else None)
                elif u in (9, 10):
                    turn(ev[:, u % 2 ^ 1], (evacuated, u), (took, 7) if u == 9 else (ya, 1))

            for u in range(1, 9):
                slots(G_IN + u * SPU, u, 0, 2, a_hi, a_lo, pair=u % 2)
                in_product(u)
                slots(G_IN + u * SPU, u, 2, SPU, a_hi, a_lo, pair=u % 2)

            def last_in(s_from, s_to):
                slots(G_IN + 9 * SPU, 9, s_from, s_to, a_hi, a_lo, pair=1)

            last_in(0, 2)
            in_product(9)
            last_in(2, 5)
            pe.wait_ge(conv, K_B * (CT - len(POOL_TILES)))
            pe.wait_ge(conv_pool, POOL_STEPS * len(POOL_TILES))
            for c in range(CT):
                mm = nc.tensor.matmul(sc[:, 0:S], mean_w[:, :], convb[:, c, :], start=c == 0,
                                      stop=c == CT - 1)
            mm.then_inc(ln_pe, 1)
            last_in(5, 7)
            pe.wait_ge(ln_act, 2)
            for tk in range(TT):
                for c in range(CT):
                    mm = nc.tensor.matmul(po[:, tk:tk + 1], sq[:, c, tk * P:(tk + 1) * P],
                                          mean_w[:, 0:1], start=c == 0, stop=c == CT - 1)
            mm.then_inc(ln_pe, 1)
            last_in(7, SPU)

            def out_slots(j, s_from, s_to, split0=None):
                g = G_OUT + (j // 2) * (2 * SPU) + (j % 2) * RING + (RING if s_from >= RING else 0)
                slots(g, U_OUT + j, s_from, s_to, b_hi, b_lo, split0=split0, pair=j % 2)

            out_slots(0, 0, 1, S_YA)
            in_product(10)
            pe.wait_ge(ln_dve, 5)
            nc.tensor.matmul(sc[:, S:2 * S], ones[:, :], dg.rearrange("p t q -> p (t q)"),
                             start=True, stop=True).then_inc(ln_pe, 1)
            out_slots(0, 1, 2, S_YA)
            out_slots(0, 2, RING, S_YA)
            out_slots(1, 0, RING)
            out_slots(0, RING, SPU, S_YA)
            out_slots(1, RING, SPU)
            for j in range(2, NCH):
                out_slots(j, 0, RING)
            for j in range(2, NCH):
                out_slots(j, RING, SPU)

            def mlp_block(b, chunks_too):
                g, u, z, sp_ = (G_MLP + b * (2 * NCH * SPU), U_MLP + b * (2 * NCH), 4 + b * NCH,
                                S_MLP + b * (2 * NCH))
                for j in range(NCH):
                    gj = g + j * SPU
                    if chunks_too and j == 0:
                        turn_residual(gj, u, [(h_ready, c + 1) for c in range(NCH)], S_N1)
                        slots(gj, u, SPU - 2, SPU, a_hi, a_lo, split0=S_N1)
                        continue
                    slots(gj, u + j, 0, 2, a_hi, a_lo, pair=j % 2)
                    if j:
                        turn(zz, (z_ready, z + j), (split_lo, sp_ + 2 * j - 3))
                    slots(gj, u + j, 2, SPU, a_hi, a_lo, pair=j % 2)
                for j in range(NCH):
                    gj = g + (NCH + j) * SPU
                    split0 = sp_ if j == 0 else None
                    slots(gj, u + (NCH + j), 0, 2, b_hi, b_lo, split0=split0, pair=j % 2)
                    if j == 0:
                        turn(zz, (z_ready, z + NCH), (split_lo, sp_ + 2 * NCH - 3))
                    slots(gj, u + (NCH + j), 2, SPU, b_hi, b_lo, split0=split0, pair=j % 2)

            mlp_block(0, True)
            with pe.Fori(1, FF1 // D) as b:
                mlp_block(b, False)

            turn_residual(G_QK, U_QK, [(h_ready, NCH + c + 1) for c in range(NCH)], S_N2)
            pe.wait_ge(split_lo, S_N2 + SPU)
            with pe.Fori(0, NCH) as i:
                for p_ in range(2):
                    g, u = G_QK + i * (2 * SPU) + p_ * SPU, U_QK + i * 2 + p_
                    slots(g, u, SPU - 2, SPU, a_hi, a_lo, pair=p_)
                    slots(g + SPU, u + 1, 0, SPU - 2, a_hi, a_lo, pair=p_ ^ 1)
                    turn(zz, (z_ready, i * 2 + (21 + p_)), (took, i * 4 + (K_QK + 2 * p_ - 1)))

            def q_of(n):
                return qkT[:, n, :]

            def k_of(n):
                return qkT[:, NH + n, :]

            def attend(n):
                if n < NH:
                    if n == 0:
                        pe.wait_ge(took, K_QK + 16)
                    else:
                        pe.wait_ge(att_dve, att_dve_at["log1" if n <= H_STICK else "logits", n - 1])
                    if n < H_STICK:
                        nc.tensor.matmul(sc[:, 0:S], k_of(n)[:, 0:P], q_of(n), start=True, stop=True)
                        mm = nc.tensor.matmul(sc[:, S:S + P], k_of(n)[:, P:S], q_of(n)[:, P:S],
                                              start=True, stop=True)
                    else:
                        nc.tensor.matmul(sc[:, 0:S], q_of(n)[:, P:S], k_of(n), start=True, stop=True)
                        mm = nc.tensor.matmul(sc[:, S:S + P], q_of(n)[:, 0:P], k_of(n)[:, 0:P],
                                              start=True, stop=True)
                    mm.then_inc(scored, 1)
                m = n - 1
                if 0 <= m < H_STICK:
                    if m == 0:
                        pe.wait_ge(consts_in, 48)
                    pe.wait_ge(att_dve, att_dve_at["masked", m])
                    after = tp[:, m % 2, :]
                    nc.tensor.matmul(after[:, 0:S], tri[:, :], x2[:, 0:S], start=True, stop=False)
                    nc.tensor.matmul(after[:, P:S], ones[:, :], x2[:, S:S + P], start=False,
                                     stop=True)
                    nc.tensor.matmul(after[:, S:S + P], tri[:, :], x2[:, S:S + P], start=True,
                                     stop=True).then_inc(turned, 1)
                elif H_STICK <= m < NH:
                    pe.wait_ge(att_dve, att_dve_at["prob", m])
                    for to, frm in ((0, S), (P, 0), (S, P)):
                        tr = nc.tensor.transpose(tp[:, m % 2, to:to + P], x2[:, frm:frm + P],
                                                 ident[:, :])
                    tr.then_inc(turned, 1)
                m = n - 2
                if m >= 0:
                    if m % 4 == 0:
                        pe.wait_ge(evacuated, U_V + m // 4 + 1)
                    if m < H_STICK:
                        pe.wait_ge(att_dve, att_dve_at["weight", m])
                    else:
                        pe.wait_ge(took, K_ATT + m - H_STICK + 1)
                    pe.wait_ge(split_lo, S_O + m)
                    nc.tensor.matmul(po[:, 0:S], vv[:, 0, m * P:(m + 1) * P], pT[:, 0:S],
                                     start=True, stop=False)
                    nc.tensor.matmul(po[:, P:S], vv[:, 1, m * P:(m + 1) * P], pT[:, S:S + P],
                                     start=False, stop=True).then_inc(valued, 1)

            for u in range(U_V, U_B0):
                g = G_V + (u - U_V) * SPU
                for s in range(SPU - 2 if u == U_V else 0, SPU):
                    slots(g, u, s, s + 1, a_hi, a_lo, pair=u % 2)
                    for n in att_points(u, s):
                        attend(n)

            def branches(g, u, ring0, pair0):
                s0 = 0
                for b, n in enumerate(BR_SLOTS):
                    slots(g + s0, u + b, 0, n, b_hi, b_lo, n=n, k0=KS * s0, ring0=ring0 + s0,
                          pair=(pair0 + b) % 2)
                    s0 += n

            pe.wait_ge(split_lo, S_O + NH)
            branches(G_B0, U_B0, 0, U_B0 % 2)
            with pe.Fori(1, NCH) as j:
                g, u = G_J - 4 * SPU + j * (4 * SPU), U_J - 6 + j * 6
                for b in range(3):
                    slots(g + b * SPU, u + b, 0, 2, a_hi, a_lo, pair=b % 2)
                    if b == 0:
                        turn(zz, (z_ready, j + 28), (split_lo, S_M - 3 + j * 2))
                    slots(g + b * SPU, u + b, 2, SPU, a_hi, a_lo, pair=b % 2)
                branches(g + 3 * SPU, u + 3, 0, 1)

            for j in range(NCH):
                split0 = S_M if j == 0 else None
                slots(G_OUT2 + j * SPU, U_OUT2 + j, 0, 2, m_hi, m_lo, split0=split0, pair=j % 2)
                if j == 0:
                    turn(zz, (z_ready, 32), (split_lo, S_M + 5))
                else:
                    turn(h[:, :, j - 1, :], (h_ready, 2 * NCH + j), (split_lo, S_N3 + 2 * j - 3))
                slots(G_OUT2 + j * SPU, U_OUT2 + j, 2, SPU, m_hi, m_lo, split0=split0, pair=j % 2)

            def ff_block(b, pairs, down_slots):
                g, u = G_FF + b * (3 * NCH * SPU), U_FF + b * (3 * NCH)
                z, sp_ = 32 + b * NCH, S_FF + b * (2 * NCH)
                for j in range(2 * pairs):
                    split0 = S_N3 if b == 0 and j == 0 else None
                    slots(g + j * SPU, u + j, 0, 2, a_hi, a_lo, split0=split0, pair=j % 2)
                    if split0 is not None:
                        turn(h[:, :, 3, :], (h_ready, 3 * NCH), (split_lo, S_N3 + 5))
                    elif j and j % 2 == 0:
                        turn(zz, (z_ready, z + j // 2), (split_lo, sp_ + j - 3))
                    slots(g + j * SPU, u + j, 2, SPU, a_hi, a_lo, split0=split0, pair=j % 2)
                gd, ud = g + 2 * pairs * SPU, u + 2 * pairs
                for j in range(NCH):
                    split0 = sp_ if j == 0 else None
                    kw = dict(split0=split0, n=down_slots, pair=j % 2, ring0=j * down_slots)
                    slots(gd + j * down_slots, ud + j, 0, 2, b_hi, b_lo, **kw)
                    if j == 0:
                        turn(zz, (z_ready, z + pairs), (split_lo, sp_ + 2 * pairs - 3))
                    slots(gd + j * down_slots, ud + j, 2, down_slots, b_hi, b_lo, **kw)

            ff_block(0, NCH, SPU)
            ff_block(1, NCH, SPU)
            ff_block(2, 3, 6)

        @block.scalar
        def _(act):
            def ticks(g0, s_from, s_to, ring0=0):
                for s in range(s_from, s_to):
                    ring = (ring0 + s) % RING
                    if isinstance(g0, int):
                        act.wait_ge(landed[ring], 16 * ((g0 + s) // RING + 1))
                        if g0 + s >= RING:
                            act.wait_ge(slot_used, g0 + s - RING + 1)
                    else:
                        act.wait_ge(landed[ring], g0 * 4 + 16 * (s // RING + 1))
                        act.wait_ge(slot_used, g0 + (s - RING + 1))
                    nc.scalar.activation(w_hi[:, ring], raw[:, ring], ACT.Copy).then_inc(hi_ready, 1)

            def evacuate(pair, used, dst, n=None, func=ACT.Copy):
                act.wait_ge(slot_used, used)
                if n is None:
                    nc.scalar.activation(dst, acc[:, pair], func).then_inc(evacuated, 1)
                    return
                for tk in range(TT):
                    a_ = nc.scalar.activation(dst[:, tk], acc[:, pair, tk], func,
                                              scale=rs[:, n, tk:tk + 1])
                a_.then_inc(evacuated, 1)

            def split(turned0, dst, k0, gain0=None):
                for g in range(2):
                    act.wait_ge(turned, turned0 + (g + 1))
                    if gain0 is None:
                        nc.scalar.activation(dst[:, bass.ds(k0 + 2 * g, 2), :].rearrange(
                            "p k s -> p (k s)"), tp[:, g, :], ACT.Copy).then_inc(split_hi, 1)
                        continue
                    for k in range(2):
                        kt = k0 + 2 * g + k
                        a_ = nc.scalar.activation(dst[:, kt, :], tp[:, g, k * S:(k + 1) * S], ACT.Copy,
                                                  scale=cols[:, gain0 + kt:gain0 + kt + 1])
                    a_.then_inc(split_hi, 1)

            def squares(n, c, src, before):
                for tk in range(TT):
                    if not (isinstance(before, int) and before + tk < 2):
                        act.wait_ge(squared, before + (tk - 1))
                    nc.scalar.activation(junk[:, tk], src[:, tk], ACT.Square,
                                         accum_out=ssq[:, n, tk, c:c + 1]).then_inc(squared, 1)

            pre = t["mix_pre_gain"][0].rearrange("(c p) -> c p", p=P)
            act.dma_start(rows[0:KT, 0, :], pre).then_inc(pre_in, 16)
            act.wait_ge(const_set, 1)
            nc.scalar.activation(den[:, :], half[:, :], ACT.Copy)

            act.wait_ge(cols_ok, 1)
            for c in range(NCH):
                split(T_X + 2 * c, a_hi, 4 * c, G_MIXPRE)
                ticks(G_IN, 2 * c, 2 * c + 2)
            for c in range(NCH):
                squares(0, c, h[:, :, c], 2 * c)

            for u in range(10):
                if u < 9:
                    ticks(G_IN + u * SPU, RING if u else SPU, RING + SPU)
                else:
                    ticks(G_IN + u * SPU, RING, RING + 5)
                    for half_ in range(2):
                        act.wait_ge(ln_dve, half_ + 1)
                        nc.scalar.activation(sq[:, 4 * half_:4 * half_ + 4, :],
                                             convb[:, 4 * half_:4 * half_ + 4, :], ACT.Square
                                             ).then_inc(ln_act, 1)
                    ticks(G_IN + u * SPU, RING + 5, RING + SPU)
                if u == 0:
                    act.wait_ge(rs_ok, 1)
                if u in (2, 4, 6, 8):
                    act.wait_ge(z_ready, u // 2)
                gates = u in (1, 3)
                evacuate(u % 2, G_IN + (u + 1) * SPU, ev[:, u % 2], 0, ACT.Sigmoid if gates else ACT.Copy)
                if u % 2 and u < 8:
                    i = u // 2
                    dst, pad, c0 = (gT, K_B - 1, 4 * i) if i < 2 else (cvT, K_A - 1, 4 * (i - 2))
                    if i in (0, 2):
                        act.wait_ge(const_set, 1)
                    for g in range(2):
                        act.wait_ge(turned, T_IN + 2 * i + g + 1)
                        nc.scalar.activation(dst[:, c0 + 2 * g:c0 + 2 * g + 2, pad:pad + S],
                                             tp[:, g, :].rearrange("p (c s) -> p c s", c=2),
                                             ACT.Copy).then_inc(took, 1)
                if u == 9:
                    ticks(G_OUT, RING, RING + 1)
                if u >= 8:
                    for g in range(2):
                        act.wait_ge(ya, 2 * (u - 8) + g + 1)
                        k0 = 4 * (u - 8) + 2 * g
                        nc.scalar.activation(b_hi[:, k0:k0 + 2, :], yt[:, g], ACT.Copy
                                             ).then_inc(split_hi, 1)

            ticks(G_OUT, RING + 1, RING + 2)
            for c in range(CT):
                if c % 4 == 0:
                    act.wait_ge(ln_dve, 6 + c // 4)
                nc.scalar.activation(yb[:, c, :], convb[:, c, :], ACT.Silu,
                                     scale=cols[:, G_LNG + c:G_LNG + c + 1],
                                     bias=cols[:, G_LNB + c:G_LNB + c + 1]).then_inc(ln_act, 1)
                if c % 2:
                    act.wait_ge(ln_act, 2 + c + 1)
                    nc.scalar.activation(b_hi[:, CT + c - 1:CT + c + 1, :], yb[:, c - 1:c + 1, :],
                                         ACT.Copy).then_inc(split_hi, 1)
                if c % 4 == 3:
                    ticks(G_OUT, RING + 2 + c // 4, RING + 3 + c // 4)

            for j in range(NCH):
                g = G_OUT + (j // 2) * (2 * SPU)
                if j % 2 == 0:
                    ticks(g, 2 * RING if j == 0 else RING, 4 * RING)
                else:
                    ticks(g, 4 * RING, 5 * RING - (j == 3))
                if j < 2:
                    act.wait_ge(ya, 4)
                else:
                    act.wait_ge(ev_read, j - 1)
                evacuate(j % 2, g + (3 + j % 2) * RING, ev[:, j % 2])
                act.wait_ge(evacuated, U_OUT + j + 1)
                squares(1, j, ev[:, j % 2], 8 + 2 * j)

            def residual(n, g, turned0, gain0, before):
                ticks(g, 3, 4)
                for c in range(NCH):
                    split(turned0 + 2 * c, a_hi, 4 * c, gain0)
                    if c >= 2:
                        ticks(g, 2 * c, 2 * c + 2)
                for c in range(NCH):
                    squares(n, c, h[:, :, c], before + 2 * c)

            residual(2, G_MLP, T_N1, G_MLPPRE, 16)

            def mlp_block(b, last=False):
                g = G_MLP + b * (2 * NCH * SPU)
                for j in range(NCH):
                    first = isinstance(b, int) and b + j == 0
                    ticks(g, RING + j * SPU + (RING if first else 0), RING + (j + 1) * SPU)
                    act.wait_ge(rs_ok, 3)
                    act.wait_ge(z_ready, b * NCH + (4 + j))
                    act.wait_ge(ev_read, b * NCH + 4)
                    evacuate(j % 2, g + (j + 1) * SPU, ev[:, j % 2], 2)
                    split(T_MLP + b * (2 * NCH) + 2 * j, b_hi, 4 * j)
                for j in range(NCH):
                    ticks(g, RING + (NCH + j) * SPU,
                          RING + (NCH + j + 1) * SPU - (last and j == NCH - 1))
                    act.wait_ge(z_ready, b * NCH + 8)
                    act.wait_ge(ev_read, b * NCH + (4 + j))
                    evacuate(j % 2, g + (NCH + j + 1) * SPU, ev[:, j % 2])
                    act.wait_ge(ev_read, b * NCH + (4 + j + 1))
                    squares(3, j, wide[:, :, j], b * (2 * NCH) + (24 + 2 * j))

            mlp_block(0)
            with act.Fori(1, FF1 // D - 1) as b:
                mlp_block(b)
            mlp_block(FF1 // D - 1, True)
            residual(4, G_QK, T_N2, G_MIX2, 56)

            with act.Fori(0, NCH) as i:
                for p_ in range(2):
                    g = G_QK + i * (2 * SPU) + p_ * SPU
                    ticks(g, SPU, SPU + RING)
                    act.wait_ge(rs_ok, 5)
                    act.wait_ge(z_ready, i * 2 + (20 + p_))
                    evacuate(p_, g + SPU, ev[:, p_], 4)
                    ticks(g, SPU + RING, 2 * SPU)
                    for q in range(2):
                        act.wait_ge(turned, T_QK + 2 * p_ + q + 1 + i * 4)
                        for k in range(2):
                            head = i * 8 + (4 * p_ + 2 * q + k)
                            a_ = nc.scalar.activation(
                                qkT[:, bass.ds(head, 1), :].rearrange("p k s -> p (k s)"),
                                tp[:, q, k * S:(k + 1) * S], ACT.Copy, scale=qkg[:, bass.ds(head, 1)])
                        a_.then_inc(took, 1)

            def attend(n):
                if 1 <= n <= H_STICK:
                    act.wait_ge(att_dve, att_dve_at["sum", n - 1])
                    nc.scalar.activation(x0[:, :], x0[:, :], ACT.Exp).then_inc(att_act, 1)
                elif H_STICK < n <= NH:
                    act.wait_ge(turned, T_ATT + n)
                    act.wait_ge(valued, n - 1)
                    nc.scalar.activation(pT[:, :], tp[:, (n - 1) % 2, 0:3 * P], ACT.Copy
                                         ).then_inc(took, 1)
                if n >= 2:
                    act.wait_ge(valued, n - 1)
                    nc.scalar.activation(b_hi[:, n - 2, :], po[:, 0:S], ACT.Copy).then_inc(split_hi, 1)
                if n < H_STICK:
                    act.wait_ge(scored, n + 1)
                    if n:
                        act.wait_ge(att_dve, att_dve_at["weight", n - 1])
                    nc.scalar.activation(x0[:, :], sc[:, 0:3 * P], ACT.Abs, scale=QSCALE
                                         ).then_inc(att_act, 1)
                    act.wait_ge(att_act, att_act_at["abs", n])
                    nc.scalar.activation(x0[:, :], x0[:, :], ACT.Exp, scale=-1.0).then_inc(att_act, 1)
                    act.wait_ge(att_act, att_act_at["exp", n])
                    nc.scalar.activation(x0[:, :], x0[:, :], ACT.Ln, bias=1.0).then_inc(att_act, 1)
                elif n < NH:
                    act.wait_ge(att_dve, att_dve_at["neg", n])
                    for i, (a_, b_) in enumerate(((0, S), (S, 3 * P))):
                        own = n < H_STICK + H_BLOCK
                        e_ = nc.scalar.activation(x1[:, a_:b_], x0[:, a_:b_], ACT.Exp,
                                                  bias=nmx[:, i:i + 1],
                                                  accum_out=den[:, i:i + 1] if own else None)
                    e_.then_inc(att_act, 1)

            for u in range(U_V, U_B0):
                g = G_V + (u - U_V) * SPU
                for s in range(RING if u == U_V else 0, SPU):
                    ticks(g, RING + s, RING + s + 1)
                    for n in att_points(u, s):
                        attend(n)
                j = u - U_V
                if j < NCH:
                    evacuate(u % 2, g + SPU, vv[:, :, j * W:(j + 1) * W], 4)
                else:
                    evacuate(u % 2, g + SPU, gate[:, j - NCH], 4)

            def merge(g, mstep0, z0, pair0):
                s0 = 0
                for b, n in enumerate(BR_SLOTS):
                    ticks(g, RING + s0, RING + s0 + n)
                    s0 += n
                    act.wait_ge(z_ready, z0)
                    if b == 2:
                        act.wait_ge(mstep, mstep0 + 1)
                    p_ = (pair0 + b) % 2
                    evacuate(p_, g + s0, ev[:, p_])

            for b in range(3):
                act.wait_ge(evacuated, U_B0)
                nc.scalar.activation(gate[:, b], gate[:, b], ACT.Sigmoid).then_inc(gated, 1)
            merge(G_B0, 0, 28, U_B0 % 2)
            with act.Fori(1, NCH) as j:
                g = G_J - 4 * SPU + j * (4 * SPU)
                for b in range(3):
                    ticks(g, RING + b * SPU, RING + b * SPU + 2)
                    if b == 0:
                        split(T_M - 2 + j * 2, m_hi, j * 4 - 4)
                    ticks(g, RING + b * SPU + 2, RING + (b + 1) * SPU)
                    act.wait_ge(z_ready, j + 28)
                    evacuate(b % 2, g + (b + 1) * SPU, gate[:, b], 4, ACT.Sigmoid)
                merge(g + 3 * SPU, j * 4, j + 28, 1)

            for j in range(NCH):
                g = G_OUT2 + j * SPU
                ticks(g, RING, RING + 2)
                if j == 0:
                    split(T_M + 6, m_hi, 12)
                ticks(g, RING + 2, RING + SPU)
                act.wait_ge(z_ready, 32)
                if j > 1:
                    act.wait_ge(h_ready, 2 * NCH + j - 1)
                evacuate(j % 2, g + SPU, ev[:, j % 2])
                split(T_N3 + 2 * j, a_hi, 4 * j, G_FFN2)
                squares(5, j, h[:, :, j], 64 + 2 * j)

            def ff_block(g, b, pairs, down_slots, last):
                z, r, tr = 32 + b * NCH, 4 + 16 + b * NCH, T_FF + b * (2 * NCH)
                for j in range(2 * pairs):
                    ticks(g, RING + j * SPU, RING + (j + 1) * SPU)
                    act.wait_ge(rs_ok, 6)
                    if j % 2 == 0:
                        act.wait_ge(z_ready, z + j // 2)
                        act.wait_ge(ev_read, r)
                    evacuate(j % 2, g + (j + 1) * SPU, ev[:, j % 2], 5,
                             ACT.Copy if j % 2 else ACT.Silu)
                    if j % 2:
                        split(tr + (j - 1), b_hi, 2 * (j - 1))
                s0 = 2 * pairs * SPU
                for j in range(NCH):
                    hi_ = RING + s0 + down_slots - (RING if last and j == NCH - 1 else 0)
                    ticks(g, RING + s0, hi_)
                    s0 += down_slots
                    act.wait_ge(z_ready, z + pairs)
                    if j > 1:
                        if last:
                            act.wait_ge(h_ready, 3 * NCH + j - 1)
                        else:
                            act.wait_ge(ev_read, r + (j - 1))
                    evacuate(j % 2, g + s0, ev[:, j % 2])

            with act.Fori(0, 2) as b:
                ff_block(G_FF + b * (3 * NCH * SPU), b, NCH, SPU, False)
            ff_block(G_FF3, 2, 3, 6, True)
        @block.vector
        def _(dve):
            def tick(g0, s, ring0=0):
                ring = (ring0 + s) % RING
                dve.wait_ge(hi_ready, g0 + (s + 1))
                nc.vector.tensor_tensor(w_lo[:, ring], raw[:, ring], w_hi[:, ring].bitcast(F32),
                                        ALU.subtract).then_inc(lo_ready, 1)

            def ticks(g0, s_from, s_to):
                for s in range(s_from, s_to):
                    tick(g0, s)

            def split(split0, hi, lo, k0, gain0=None):
                for g in range(2):
                    dve.wait_ge(split_hi, split0 + (g + 1))
                    if gain0 is None:
                        hi_, lo_ = (x[:, bass.ds(k0 + 2 * g, 2), :].rearrange("p k s -> p (k s)")
                                    for x in (hi, lo))
                        nc.vector.tensor_tensor(lo_, tp[:, g, :], hi_.bitcast(F32), ALU.subtract
                                                ).then_inc(split_lo, 1)
                        continue
                    for k in range(2):
                        kt = k0 + 2 * g + k
                        v = nc.vector.scalar_tensor_tensor(
                            lo[:, kt, :], tp[:, g, k * S:(k + 1) * S],
                            cols[:, gain0 + kt:gain0 + kt + 1], hi[:, kt, :].bitcast(F32),
                            ALU.mult, ALU.subtract)
                    v.then_inc(split_lo, 1)

            def mean_square(n, count):
                dve.wait_ge(squared, count)
                nc.vector.reduce_sum(ms[:, n, :], ssq[:, n], AX.X).then_inc(ssum, 1)
                dve.wait_ge(ssum, 2 * n + 1)
                nc.vector.tensor_scalar(ms[:, n, :], ms[:, n, :], 1.0 / D, EPS, ALU.mult, ALU.add
                                        ).then_inc(ssum, 1)

            nc.vector.memset(qkg[:, :], 1.0).then_inc(step0, 1)
            dve.wait_ge(cols_T, 1)
            nc.vector.tensor_copy(cols[:, 0:KT], sc[:, 0:KT]).then_inc(cols_ok, 1)
            dve.wait_ge(cols_ok, 1)

            for c in range(NCH):
                split(S_X + 2 * c, a_hi, a_lo, 4 * c, G_MIXPRE)
                ticks(G_IN, 2 * c, 2 * c + 2)
            mean_square(0, 8)

            def taps_long():
                n = 0
                for half_ in range(2):
                    for k in range(K_B):
                        for c in range(4 * half_, 4 * half_ + 3):
                            if k == 0 and c % 4 == 0:
                                dve.wait_ge(took, 4 * half_ // 2 + 2)
                            if k:
                                dve.wait_ge(conv, n - 2)
                            if k == 0:
                                tap_first(nc.vector, c).then_inc(conv, 1)
                            else:
                                nc.vector.scalar_tensor_tensor(convb[:, c, :], gT[:, c, k:k + S],
                                                               tap_weight(c, k), convb[:, c, :],
                                                               ALU.mult, ALU.add).then_inc(conv, 1)
                            n += 1
                            yield

            long_ = taps_long()

            def over_channels(half_, row, op):
                part = convb[:, 4 * half_:4 * half_ + 4, :]
                return nc.vector.tensor_tensor(part, part, row.unsqueeze(1).to_broadcast([P, 4, S]), op)

            for u in range(10):
                for s in range(0 if u else RING, SPU):
                    if u == 9 and s == 5:
                        for _ in long_:
                            pass
                        dve.wait_ge(ln_pe, 1)
                        for half_ in range(2):
                            over_channels(half_, sc[:, 0:S], ALU.subtract).then_inc(ln_dve, 1)
                    if u == 9 and s == 7:
                        dve.wait_ge(ln_pe, 2)
                        nc.vector.tensor_scalar(lnv[:, :], po[:, 0:TT], EPS, None, ALU.add
                                                ).then_inc(ln_dve, 1)
                    tick(G_IN + u * SPU, RING + s)
                    if u >= 2:
                        for _ in range(3 + (s % 4 == 3)):
                            next(long_, None)
                if u == 0:
                    dve.wait_ge(cols_T, 2)
                    nc.vector.tensor_copy(cols[:, KT:3 * P], sc[:, KT:3 * P]).then_inc(cols_ok, 1)
                    dve.wait_ge(cols_ok, 2)
                    dve.wait_ge(step0, 1)
                    nc.vector.tensor_copy(qkg[:, H_STICK:NH], cols[:, G_QG:G_QG + H_SOFT]
                                          ).then_inc(step0, 1)
                    nc.vector.tensor_copy(qkg[:, NH + H_STICK:2 * NH], cols[:, G_KG:G_KG + H_SOFT]
                                          ).then_inc(step0, 1)
                    dve.wait_ge(cols_T, 3)
                    nc.vector.tensor_tensor(line[:, :], po[0:H_SOFT, 0:LINE], lmask[:, :], ALU.add
                                            ).then_inc(cols_ok, 1)
                if u % 2 and u < 8:
                    dve.wait_ge(evacuated, u + 1)
                    if u > 1:
                        dve.wait_ge(turned, T_IN + u - 1)
                    nc.vector.tensor_tensor(zz[:, :, :], ev[:, 0], ev[:, 1], ALU.mult
                                            ).then_inc(z_ready, 1)
                if u == 9:
                    dve.wait_ge(ln_pool, 1)
                    for tk in range(TT):
                        nc.vector.tensor_scalar(dg[:, tk, :], ident[:, :], lnr[:, tk:tk + 1], None,
                                                ALU.mult).then_inc(ln_dve, 1)
                    tick(G_OUT, RING)
                if u >= 8:
                    for g in range(2):
                        dve.wait_ge(turned, T_IN + u + (u - 8) + g + 1)
                        c0 = 4 * (u - 8) + 2 * g
                        if g == 0:
                            dve.wait_ge(conv3, (2 * K_A - 1) * (u - 7))
                        if u == 9:
                            dve.wait_ge(split_lo, S_YA + g + 1)
                        nc.vector.tensor_tensor(
                            yt[:, g], tp[:, g, :].rearrange("p (c s) -> p c s", c=2),
                            conva[:, c0:c0 + 2, :], ALU.mult).then_inc(ya, 1)
                    for g in range(2):
                        c0 = 4 * (u - 8) + 2 * g
                        dve.wait_ge(split_hi, S_YA + 2 * (u - 8) + g + 1)
                        nc.vector.tensor_tensor(b_lo[:, c0:c0 + 2, :], yt[:, g],
                                                b_hi[:, c0:c0 + 2, :].bitcast(F32), ALU.subtract
                                                ).then_inc(split_lo, 1)
            dve.wait_ge(ln_pe, 3)
            for half_ in range(2):
                over_channels(half_, sc[:, S:2 * S], ALU.mult).then_inc(ln_dve, 1)
            tick(G_OUT, RING + 1)
            for c in range(0, CT, 2):
                dve.wait_ge(split_hi, S_YB + c // 2 + 1)
                nc.vector.tensor_tensor(b_lo[:, CT + c:CT + c + 2, :], yb[:, c:c + 2, :],
                                        b_hi[:, CT + c:CT + c + 2, :].bitcast(F32), ALU.subtract
                                        ).then_inc(split_lo, 1)
                if c % 4 == 2:
                    tick(G_OUT, RING + 2 + c // 4)

            dve.wait_ge(gain1_in, 16)
            for j in range(NCH):
                g = G_OUT + (j // 2) * (2 * SPU)
                if j % 2 == 0:
                    ticks(g, 2 * RING if j == 0 else RING, 4 * RING)
                else:
                    ticks(g, 4 * RING, 5 * RING - (j == 3))
                dve.wait_ge(evacuated, U_OUT + j + 1)
                row = gain[:, j * W:(j + 1) * W].unsqueeze(1).to_broadcast([P, TT, W])
                nc.vector.tensor_tensor(wide[:, :, j], ev[:, j % 2], row, ALU.mult
                                        ).then_inc(ev_read, 1)

            def gained(c):
                row = gain[:, c * W:(c + 1) * W].unsqueeze(1).to_broadcast([P, TT, W])
                nc.vector.tensor_tensor(wide[:, :, c], wide[:, :, c], row, ALU.mult
                                        ).then_inc(qstep, 1)

            def residual(n, g, split0, gain0, gain_too):
                dve.wait_ge(rs_ok, n + 1)
                for c in range(NCH + 1):
                    if c < NCH:
                        if gain_too:
                            dve.wait_ge(qstep, c + 1)
                        for tk in range(TT):
                            v = nc.vector.scalar_tensor_tensor(h[:, tk, c], wide[:, tk, c],
                                                               rs[:, n, tk:tk + 1], h[:, tk, c],
                                                               ALU.mult, ALU.add)
                        v.then_inc(h_ready, 1)
                        if gain_too and c == 1:
                            gained(3)
                    if c:
                        split(split0 + 2 * c - 2, a_hi, a_lo, 4 * c - 4, gain0)
                    if c == 1:
                        ticks(g, 3, 4)
                    if c >= 3:
                        ticks(g, 2 * c - 2, 2 * c)

            mean_square(1, 16)
            dve.wait_ge(ev_read, NCH)
            residual(1, G_MLP, S_N1, G_MLPPRE, False)
            mean_square(2, 24)

            def mlp_block(b, last=False):
                g, u = G_MLP + b * (2 * NCH * SPU), U_MLP + b * (2 * NCH)
                for j in range(NCH):
                    first = isinstance(b, int) and b + j == 0
                    ticks(g, RING + j * SPU + (RING if first else 0), RING + (j + 1) * SPU)
                    dve.wait_ge(evacuated, u + (j + 1))
                    dve.wait_ge(turned, T_MLP + b * (2 * NCH) + 2 * j)
                    nc.vector.scalar_tensor_tensor(zz[:, :, :], ev[:, j % 2], 0.0, ev[:, j % 2],
                                                   ALU.max, ALU.mult).then_inc(z_ready, 1)
                    split(S_MLP + b * (2 * NCH) + 2 * j, b_hi, b_lo, 4 * j)
                if isinstance(b, int) and b == 0:
                    dve.wait_ge(wide_zero, 1)
                for j in range(NCH):
                    ticks(g, RING + (NCH + j) * SPU,
                          RING + (NCH + j + 1) * SPU - (last and j == NCH - 1))
                    if last and j:
                        dve.wait_ge(squared, b * (2 * NCH) + (24 + 2 * j))
                        gained(j - 1)
                    dve.wait_ge(evacuated, u + (NCH + j + 1))
                    dve.wait_ge(squared, b * (2 * NCH) + (18 + 2 * j))
                    nc.vector.tensor_tensor(wide[:, :, j], wide[:, :, j], ev[:, j % 2], ALU.add
                                            ).then_inc(ev_read, 1)

            mlp_block(0)
            with dve.Fori(1, FF1 // D - 1) as b:
                mlp_block(b)
            dve.wait_ge(gain2_in, 16)
            mlp_block(FF1 // D - 1, True)
            mean_square(3, 56)
            residual(3, G_QK, S_N2, G_MIX2, True)
            mean_square(4, 64)

            with dve.Fori(0, NCH) as i:
                for p_ in range(2):
                    g = G_QK + i * (2 * SPU) + p_ * SPU
                    ticks(g, SPU, SPU + RING)
                    dve.wait_ge(evacuated, U_QK + p_ + 1 + i * 2)
                    dve.wait_ge(turned, T_QK + 2 * p_ + i * 4)
                    heads = zz.rearrange("p t (g d) -> p (t g) d", d=P)
                    v0 = i * 6 + (NCH + 3 * p_)
                    nc.vector.tensor_tensor(zz[:, :, :], ev[:, p_], ev[:, p_], ALU.mult
                                            ).then_inc(qstep, 1)
                    dve.wait_ge(qstep, v0 + 1)
                    nc.vector.reduce_sum(qss[:, :], heads, AX.X).then_inc(qstep, 1)
                    dve.wait_ge(qstep, v0 + 2)
                    nc.vector.tensor_scalar(qms[:, :], qss[:, :], 1.0 / P, EPS, ALU.mult, ALU.add
                                            ).then_inc(qstep, 1)
                    tick(g, SPU + RING)
                    dve.wait_ge(qpool, i * 2 + (p_ + 1))
                    nc.vector.tensor_tensor(heads, ev[:, p_].rearrange("p t (g d) -> p (t g) d", d=P),
                                            qrs[:, :].unsqueeze(2).to_broadcast([P, 8, P]), ALU.mult
                                            ).then_inc(z_ready, 1)
                    ticks(g, SPU + RING + 1, 2 * SPU)

            def attend(n):
                def step(v):
                    v.then_inc(att_dve, 1)

                def behind(stage, m):
                    dve.wait_ge(att_dve, att_dve_at[stage, m])

                parts = ((0, S), (S, 3 * P))
                if n == 0:
                    dve.wait_ge(consts_in, 48)
                if 1 <= n <= H_STICK:
                    dve.wait_ge(turned, T_ATT + n)
                    step(nc.vector.tensor_tensor(x0[:, :], x1[:, :], tp[:, (n - 1) % 2, 0:3 * P],
                                                 ALU.add))
                if n >= 2:
                    dve.wait_ge(split_hi, S_O + n - 1)
                    nc.vector.tensor_tensor(b_lo[:, n - 2, :], po[:, 0:S],
                                            b_hi[:, n - 2, :].bitcast(F32), ALU.subtract
                                            ).then_inc(split_lo, 1)
                if 1 <= n <= H_STICK:
                    dve.wait_ge(att_act, att_act_at["weight", n - 1])
                    if n > 1:
                        dve.wait_ge(valued, n - 1)
                    for a_, b_ in parts:
                        step(nc.vector.tensor_tensor(pT[:, a_:b_], x0[:, a_:b_], past[:, 0:b_ - a_],
                                                     ALU.mult))
                if n < H_STICK:
                    dve.wait_ge(scored, n + 1)
                    dve.wait_ge(att_act, att_act_at["log", n])
                    step(nc.vector.tensor_scalar(x1[:, :], sc[:, 0:3 * P], QSCALE, 0.0, ALU.mult,
                                                 ALU.min))
                    behind("min", n)
                    step(nc.vector.tensor_tensor(x1[:, :], x1[:, :], x0[:, :], ALU.subtract))
                    behind("logb", n)
                    step(nc.vector.scalar_tensor_tensor(x2[:, :], sc[:, 0:3 * P], -QSCALE, x1[:, :],
                                                        ALU.mult, ALU.add))
                    behind("log1", n)
                    for a_, b_ in parts:
                        step(nc.vector.tensor_tensor(x2[:, a_:b_], x2[:, a_:b_], past[:, 0:b_ - a_],
                                                     ALU.mult))
                elif n < NH:
                    m = n - H_STICK
                    bias_ = bias[:, m % 2, :]
                    if n == H_STICK:
                        behind("weight", n - 1)
                    dve.wait_ge(scored, n + 1)
                    dve.wait_ge(bias_in[m % 2], 16 * (m // 2 + 1))
                    for (a_, b_), tab in zip(parts, (bias_, bias_[:, P:S])):
                        step(nc.vector.scalar_tensor_tensor(x0[:, a_:b_], sc[:, a_:b_], QSCALE, tab,
                                                            ALU.mult, ALU.add))
                    behind("logits", n)
                    for i, (a_, b_) in enumerate(parts):
                        step(nc.vector.reduce_max(mx[:, i:i + 1], x0[:, a_:b_], AX.X))
                    behind("max", n)
                    step(nc.vector.tensor_scalar(nmx[:, :], mx[:, :], -1.0, None, ALU.mult))
                    dve.wait_ge(att_act, att_act_at["exp", n])
                    if m >= H_BLOCK:
                        for i, (a_, b_) in enumerate(parts):
                            step(nc.vector.scalar_tensor_tensor(
                                x1[:, a_:b_], x1[:, a_:b_], 1.0, cnt[:, a_:b_], ALU.mult, ALU.mult,
                                accum_out=den[:, i:i + 1]))
                        behind("count", n)
                    step(nc.vector.reciprocal(rden[:, :], den[:, :]))
                    behind("recip", n)
                    dve.wait_ge(turned, T_ATT + n)
                    for i, (a_, b_) in enumerate(parts):
                        step(nc.vector.tensor_scalar(x2[:, a_:b_], x1[:, a_:b_], rden[:, i:i + 1],
                                                     None, ALU.mult))

            for u in range(U_V, U_B0):
                for s in range(RING if u == U_V else 0, SPU):
                    tick(G_V + (u - U_V) * SPU, RING + s)
                    for n in att_points(u, s):
                        attend(n)

            def merge(g, u, mstep0, pair0):
                s0 = 0
                for b, n in enumerate(BR_SLOTS):
                    ticks(g, RING + s0, RING + s0 + n)
                    s0 += n
                    e_ = ev[:, (pair0 + b) % 2]
                    dve.wait_ge(evacuated, u + (b + 1))
                    if b == 0:
                        nc.vector.tensor_tensor(zz[:, :, :], gate[:, b], e_, ALU.mult
                                                ).then_inc(mstep, 1)
                        continue
                    nc.vector.tensor_tensor(e_, gate[:, b], e_, ALU.mult).then_inc(mstep, 1)
                    dve.wait_ge(mstep, mstep0 + 2 * b)
                    v = nc.vector.tensor_tensor(zz[:, :, :], zz[:, :, :], e_, ALU.add)
                    v.then_inc(*((z_ready, 1) if b == 2 else (mstep, 1)))

            dve.wait_ge(gated, 3)
            merge(G_B0, U_B0, 0, U_B0 % 2)
            with dve.Fori(1, NCH) as j:
                g, u = G_J - 4 * SPU + j * (4 * SPU), U_J - 6 + j * 6
                for b in range(3):
                    ticks(g, RING + b * SPU, RING + b * SPU + 2)
                    if b == 0:
                        split(S_M - 2 + j * 2, m_hi, m_lo, j * 4 - 4)
                    ticks(g, RING + b * SPU + 2, RING + (b + 1) * SPU)
                merge(g + 3 * SPU, u + 3, j * 4, 1)

            for j in range(NCH):
                g = G_OUT2 + j * SPU
                ticks(g, RING, RING + 2)
                if j == 0:
                    split(S_M + 6, m_hi, m_lo, 12)
                ticks(g, RING + 2, RING + SPU)
                dve.wait_ge(evacuated, U_OUT2 + j + 1)
                nc.vector.tensor_tensor(h[:, :, j], h[:, :, j], ev[:, j % 2], ALU.add
                                        ).then_inc(h_ready, 1)
                split(S_N3 + 2 * j, a_hi, a_lo, 4 * j, G_FFN2)
            mean_square(5, 72)

            def ff_block(g, u, b, pairs, down_slots, last):
                for j in range(2 * pairs):
                    ticks(g, RING + j * SPU, RING + (j + 1) * SPU)
                    if last and 1 <= j <= NCH:
                        nc.vector.tensor_tensor(h[:, :, j - 1], h[:, :, j - 1], wide[:, :, j - 1],
                                                ALU.add).then_inc(folded, 1)
                    if j % 2 == 0:
                        continue
                    dve.wait_ge(evacuated, u + (j + 1))
                    dve.wait_ge(turned, T_FF + b * (2 * NCH) + (j - 1))
                    nc.vector.tensor_tensor(zz[:, :, :], ev[:, 0], ev[:, 1], ALU.mult
                                            ).then_inc(z_ready, 1)
                    split(S_FF + b * (2 * NCH) + (j - 1), b_hi, b_lo, 2 * (j - 1))
                s0 = 2 * pairs * SPU
                for j in range(NCH):
                    ticks(g, RING + s0,
                          RING + s0 + down_slots - (RING if last and j == NCH - 1 else 0))
                    s0 += down_slots
                    dve.wait_ge(evacuated, u + (2 * pairs + j + 1))
                    if last:
                        dve.wait_ge(folded, j + 1)
                        nc.vector.tensor_tensor(h[:, :, j], h[:, :, j], ev[:, j % 2], ALU.add
                                                ).then_inc(h_ready, 1)
                    else:
                        nc.vector.tensor_tensor(wide[:, :, j], wide[:, :, j], ev[:, j % 2], ALU.add
                                                ).then_inc(ev_read, 1)

            dve.wait_ge(wide_zero, 2)
            with dve.Fori(0, 2) as b:
                ff_block(G_FF + b * (3 * NCH * SPU), U_FF + b * (3 * NCH), b, NCH, SPU, False)
            ff_block(G_FF3, U_FF + 6 * NCH, 2, 3, 6, True)

        @block.gpsimd
        def _(pool):
            nc.gpsimd.memset(mean_w[:, :], 1.0 / D_A)
            nc.gpsimd.memset(ones[:, :], 1.0)
            nc.gpsimd.memset(half[:, :], -0.5)
            nc.gpsimd.memset(qexp[:, :, :], -0.5)
            nc.gpsimd.memset(gT[:, :, 0:K_B - 1], 0.0)
            nc.gpsimd.memset(cvT[:, :, 0:K_A - 1], 0.0).then_inc(const_set, 1)
            pool.wait_ge(const_set, 1)
            nc.gpsimd.memset(qexp[:, 0:8:4, :], 0.0).then_inc(const_set, 1)

            def root(n):
                pool.wait_ge(ssum, 2 * n + 2)
                nc.gpsimd.tensor_tensor(rs[:, n, :], ms[:, n, :], half[:, :], ALU.pow
                                        ).then_inc(rs_ok, 1)

            root(0)
            pool.wait_ge(cols_ok, 3)
            pool.dma_start(line_dram, line[:, :]).then_inc(line_out, 16)
            for i in range(SKEWS):
                m = slice(i * (H_SOFT // SKEWS), (i + 1) * (H_SOFT // SKEWS))
                pool.wait_ge(line_out, 16 * (i + 1))
                pool.dma_start(t["skew_dram"][m], line_dram[m].unsqueeze(1).to_broadcast(
                    [H_SOFT // SKEWS, P, LINE])).then_inc(line_out, 16)

            pool.dma_start(gain[:, :], bass.AP(t["mix_post_gain"].tensor, 0, [[0, P], [1, D]])
                           ).then_inc(gain1_in, 16)
            for i, c in enumerate(POOL_TILES):
                pool.wait_ge(took, 2 * i + 2)
                done = i * POOL_STEPS
                if i:
                    pool.wait_ge(conv_pool, done)
                tap_first(nc.gpsimd, c).then_inc(conv_pool, 1)
                for k in range(1, K_B + 1):
                    if k < K_B:
                        if k > 4:
                            pool.wait_ge(conv_pool, done + 2 * k - 6)
                        nc.gpsimd.tensor_scalar(prod[:, k % 4], gT[:, c, k:k + S], tap_weight(c, k),
                                                None, ALU.mult).then_inc(conv_pool, 1)
                    if k > 1:
                        pool.wait_ge(conv_pool, done + 2 * k - 2)
                        nc.gpsimd.tensor_tensor(convb[:, c, :], convb[:, c, :],
                                                prod[:, (k - 1) % 4], ALU.add
                                                ).then_inc(conv_pool, 1)
            pool.wait_ge(line_out, 16 * (SKEWS + 1))
            pool.wait_ge(conv_pool, 2 * POOL_STEPS)
            for half_ in range(2):
                pool.wait_ge(took, 4 + 2 * half_ + 2)
                sums = conva[:, 4 * half_:4 * half_ + 4, :]
                for k in range(K_A):
                    done = (half_ * (2 * K_A - 1)) + max(2 * k - 1, 0)
                    if done:
                        pool.wait_ge(conv3, done)
                    for q in range(4):
                        c = 4 * half_ + q
                        w_ = cols[:, G_CONVA + CT * k + c:G_CONVA + CT * k + c + 1]
                        v = nc.gpsimd.tensor_scalar(prod[:, q] if k else sums[:, q],
                                                    cvT[:, c, k:k + S], w_, None, ALU.mult)
                    v.then_inc(conv3, 1)
                    if k:
                        pool.wait_ge(conv3, done + 1)
                        nc.gpsimd.tensor_tensor(sums, sums, prod[:, :, :], ALU.add
                                                ).then_inc(conv3, 1)

            pool.wait_ge(ln_dve, 3)
            nc.gpsimd.tensor_tensor(lnr[:, :], lnv[:, :], half[:, :], ALU.pow).then_inc(ln_pool, 1)
            root(1)
            pool.wait_ge(h_ready, NCH)
            nc.gpsimd.memset(wide[:, :, :, :], 0.0).then_inc(wide_zero, 1)
            pool.dma_start(gain[:, :], bass.AP(t["mlp_post_gain"].tensor, 0, [[0, P], [1, D]])
                           ).then_inc(gain2_in, 16)
            root(2)
            root(3)
            root(4)
            with pool.Fori(0, NCH) as i:
                for p_ in range(2):
                    pool.wait_ge(qstep, i * 6 + (NCH + 3 * p_ + 3))
                    nc.gpsimd.tensor_tensor(
                        qrs[:, :], qms[:, :],
                        qexp[:, bass.ds(i * 2 + p_, 1), :].rearrange("p u g -> p (u g)"),
                        ALU.pow).then_inc(qpool, 1)

            pool.wait_ge(turned, T_ATT)
            pool.dma_start(cnt[:, :], t["cnt"]).then_inc(consts_in, 16)
            pool.dma_start(past[:, :], t["past"]).then_inc(consts_in, 16)
            pool.dma_start(tri[:, :], t["tri"]).then_inc(consts_in, 16)
            pool.wait_ge(line_out, 16 * (SKEWS + 1))
            for m in range(H_SOFT):
                if m >= 2:
                    pool.wait_ge(att_dve, att_dve_at["logits", H_STICK + m - 2])
                src = bass.AP(t["skew_dram"].tensor, m * P * LINE + P - 1, [[LINE - 1, P], [1, S]])
                pool.dma_start(bias[:, m % 2, :], src).then_inc(bias_in[m % 2], 16)
            pool.wait_ge(evacuated, U_B0 + 1)
            nc.gpsimd.memset(wide[:, :, :, :], 0.0).then_inc(wide_zero, 1)
            root(5)


def tables():
    dist = 255 - np.arange(LINE)
    d = np.maximum(dist, 1).astype(np.float64)
    far = np.minimum(16 + np.floor(np.log(d / 16) / np.log(2048 / 16) * 16).astype(np.int64), 31)
    bucket = np.where(dist < 16, np.maximum(dist, 0), far)
    onehot = (np.arange(32)[:, None] == bucket[None, :]).astype(np.float32)

    def patterns(x):
        return ((x >= 0) * 1 * (x <= 128) + ((x >= 0) & (x % 4 == 0)) + ((x >= 0) & (x % 16 == 0)))

    lmask = np.zeros((H_SOFT, LINE), np.float32)
    lmask[:H_BLOCK, dist < 0] = -1e30
    lmask[H_BLOCK:, patterns(dist) == 0] = -1e30
    p = np.arange(P)[:, None]
    cnt = np.concatenate([patterns(P + p - np.arange(S)[None]), patterns(p - np.arange(P)[None])], 1)
    return {"ident": np.eye(P, dtype=np.float32), "onehot": onehot, "lmask": lmask,
            "cnt": cnt.astype(np.float32), "past": (np.arange(S)[None] > p).astype(np.float32),
            "tri": (p > np.arange(P)[None]).astype(np.float32)}


NAMES = ["x", "mix_pre_gain", "w_in", "conv_a_w", "conv_b_w", "conv_b_bias", "ln_b_gain", "ln_b_bias",
         "w_out", "mix_post_gain", "mlp_pre_gain", "w_up", "w_down", "mlp_post_gain", "g_mix_2",
         "w_in_2", "q_gain_2", "k_gain_2", "w_branch_2", "w_out_2", "g_ffn_2", "w_gu_2", "w_down_2",
         "rel_bias_2"]


def kernel(**inputs):
    import concourse.bacc as bacc
    from concourse.bass_utils import run_bass_kernel_spmd

    nc = bacc.Bacc("TRN2", target_bir_lowering=False, num_devices=1)
    arrays, args = {}, {}
    for name, value in [(n, inputs[n]) for n in NAMES] + list(tables().items()):
        a = np.ascontiguousarray(value)
        arrays[name + "_dram"] = a
        args[name] = nc.dram_tensor(name + "_dram", a.shape, mybir.dt.from_np(a.dtype),
                                    kind="ExternalInput").ap()
    args["out"] = nc.dram_tensor("out_dram", (1, S, D), F32, kind="ExternalOutput").ap()
    args["line_dram"] = nc.dram_tensor("line_dram", (H_SOFT, LINE), F32, kind="Internal").ap()
    args["skew_dram"] = nc.dram_tensor("skew_dram", (H_SOFT, P, LINE), F32, kind="Internal").ap()
    build_program(nc, args)
    result = run_bass_kernel_spmd(nc, [arrays], core_ids=[0])
    return result.results[0]["out_dram"]
```
